# Optimizing a Trainium2 kernel written in Bass

```python
import jax, jax.numpy as jnp
from jax import lax
import numpy as np

D_MODEL = 1024
BATCH = 1
SEQ = 512
DEPTH = 2

CHUNK = 64
N_META = 16
HEAD_DIM = 64
N_Q_HEADS = D_MODEL // HEAD_DIM
N_KV_HEADS = N_Q_HEADS // 4
GROUP = N_Q_HEADS // N_KV_HEADS
WINDOW = 128
WINDOW_CHUNKS = WINDOW // CHUNK
CONV_CH = D_MODEL
CONV_K = 31
D_FF = ((8 * D_MODEL // 3 + 127) // 128) * 128
Q_W = N_Q_HEADS * HEAD_DIM
KV_W = N_KV_HEADS * HEAD_DIM
P_IN = 2 * CONV_CH + Q_W + 2 * KV_W + 2 * D_MODEL
EPS = 1e-6
NEG = -1e30

kernel_name = "hybrid_conformer_swa_sink_meta"

def rms_norm(x, g):
    xf = x.astype(jnp.float32)
    y = xf * lax.rsqrt(jnp.mean(xf * xf, axis=-1, keepdims=True) + EPS)
    return (y * g.astype(jnp.float32)).astype(x.dtype)

def layer_norm(x, g, b):
    xf = x.astype(jnp.float32)
    mu = jnp.mean(xf, axis=-1, keepdims=True)
    var = jnp.mean(jnp.square(xf - mu), axis=-1, keepdims=True)
    y = (xf - mu) * lax.rsqrt(var + EPS)
    return (y * g.astype(jnp.float32) + b.astype(jnp.float32)).astype(x.dtype)

def swiglu(h, w_in, w_out):
    gu = h @ w_in
    gate, up = gu[..., :D_FF], gu[..., D_FF:]
    return (jax.nn.silu(gate) * up) @ w_out

def conv_module(u_in, conv_w, conv_b, ln_g, ln_b, w_proj):
    a, b = u_in[..., :CONV_CH], u_in[..., CONV_CH:]
    u = a * jax.nn.sigmoid(b)
    u = lax.conv_general_dilated(
        u, conv_w[:, None, :], window_strides=(1,), padding=[(CONV_K - 1, 0)],
        dimension_numbers=("NWC", "WIO", "NWC"), feature_group_count=CONV_CH) + conv_b
    u = jax.nn.silu(layer_norm(u, ln_g, ln_b))
    return u @ w_proj

def _shift_chunks(t, s):
    if s == 0:
        return t
    return jnp.concatenate([jnp.zeros_like(t[:, :s]), t[:, :-s]], axis=1)

def _sink_softmax(s, sink):
    sink_b = jnp.broadcast_to(sink.astype(jnp.float32), s.shape[:-1] + (1,))
    p = jax.nn.softmax(jnp.concatenate([s, sink_b], axis=-1), axis=-1)
    return p[..., :-1]

def window_sink_attention(q, k, v, sinks):
    B, L = q.shape[0], q.shape[1]
    n_chunks = (L - N_META) // CHUNK
    scale = HEAD_DIM ** -0.5
    sink = sinks.reshape(N_KV_HEADS, GROUP)[..., None, None]
    km, vm = k[:, :N_META], v[:, :N_META]

    qr = q[:, N_META:].reshape(B, n_chunks, CHUNK, N_KV_HEADS, GROUP, HEAD_DIM)
    kr = k[:, N_META:].reshape(B, n_chunks, CHUNK, N_KV_HEADS, HEAD_DIM)
    vr = v[:, N_META:].reshape(B, n_chunks, CHUNK, N_KV_HEADS, HEAD_DIM)
    shifts = list(range(WINDOW_CHUNKS - 1, -1, -1))
    meta_b = lambda t: jnp.broadcast_to(t[:, None], (B, n_chunks) + t.shape[1:])
    keys = jnp.concatenate([meta_b(km)] + [_shift_chunks(kr, s) for s in shifts], axis=2)
    vals = jnp.concatenate([meta_b(vm)] + [_shift_chunks(vr, s) for s in shifts], axis=2)
    cidx = jnp.arange(n_chunks)
    valid = jnp.concatenate(
        [jnp.ones((n_chunks, N_META), bool)]
        + [jnp.broadcast_to((cidx >= s)[:, None], (n_chunks, CHUNK)) for s in shifts], axis=1)
    s_r = jnp.einsum("bnqhgd,bnkhd->bnhgqk", qr, keys,
                     preferred_element_type=jnp.float32) * scale
    s_r = jnp.where(valid[None, :, None, None, None, :], s_r, NEG)
    p_r = _sink_softmax(s_r, sink).astype(v.dtype)
    o_r = jnp.einsum("bnhgqk,bnkhd->bnqhgd", p_r, vals).reshape(B, n_chunks * CHUNK, Q_W)

    qm = q[:, :N_META].reshape(B, N_META, N_KV_HEADS, GROUP, HEAD_DIM)
    s_m = jnp.einsum("bqhgd,bkhd->bhgqk", qm, km, preferred_element_type=jnp.float32) * scale
    p_m = _sink_softmax(s_m, sink).astype(v.dtype)
    o_m = jnp.einsum("bhgqk,bkhd->bqhgd", p_m, vm).reshape(B, N_META, Q_W)
    return jnp.concatenate([o_m, o_r], axis=1)

def setup_inputs(seed: int = 0) -> dict:
    key = jax.random.key(seed)
    ks = jax.random.split(key, 24)
    nrm = lambda k, shape, s: jax.random.normal(k, shape, jnp.float32) * s
    gain = lambda k, shape: 1.0 + nrm(k, shape, 0.05)
    return {
        "x": nrm(ks[0], (BATCH, SEQ, D_MODEL), 1.0),
        "meta_tokens": nrm(ks[1], (N_META, D_MODEL), 1.0),
        "ffn1_norm": gain(ks[2], (DEPTH, D_MODEL)),
        "ffn1_w_in": nrm(ks[3], (DEPTH, D_MODEL, 2 * D_FF), D_MODEL ** -0.5),
        "ffn1_w_out": nrm(ks[4], (DEPTH, D_FF, D_MODEL), D_FF ** -0.5),
        "mix_norm": gain(ks[5], (DEPTH, D_MODEL)),
        "w_in": nrm(ks[6], (DEPTH, D_MODEL, P_IN), D_MODEL ** -0.5),
        "gate_bias": nrm(ks[7], (DEPTH, 2 * D_MODEL), 0.02),
        "conv_w": nrm(ks[8], (DEPTH, CONV_K, CONV_CH), CONV_K ** -0.5),
        "conv_b": nrm(ks[9], (DEPTH, CONV_CH), 0.02),
        "conv_ln_g": gain(ks[10], (DEPTH, CONV_CH)),
        "conv_ln_b": nrm(ks[11], (DEPTH, CONV_CH), 0.02),
        "conv_w_out": nrm(ks[12], (DEPTH, CONV_CH, D_MODEL), CONV_CH ** -0.5),
        "q_norm": gain(ks[13], (DEPTH, HEAD_DIM)),
        "k_norm": gain(ks[14], (DEPTH, HEAD_DIM)),
        "attn_sinks": nrm(ks[15], (DEPTH, N_Q_HEADS), 0.5),
        "attn_w_out": nrm(ks[16], (DEPTH, Q_W, D_MODEL), Q_W ** -0.5),
        "w_out": nrm(ks[17], (DEPTH, D_MODEL, D_MODEL), D_MODEL ** -0.5),
        "ffn2_norm": gain(ks[18], (DEPTH, D_MODEL)),
        "ffn2_w_in": nrm(ks[19], (DEPTH, D_MODEL, 2 * D_FF), D_MODEL ** -0.5),
        "ffn2_w_out": nrm(ks[20], (DEPTH, D_FF, D_MODEL), D_FF ** -0.5),
    }

def reference(x, meta_tokens, ffn1_norm, ffn1_w_in, ffn1_w_out, mix_norm, w_in, gate_bias,
              conv_w, conv_b, conv_ln_g, conv_ln_b, conv_w_out, q_norm, k_norm, attn_sinks,
              attn_w_out, w_out, ffn2_norm, ffn2_w_in, ffn2_w_out):
    B = x.shape[0]
    meta = jnp.broadcast_to(meta_tokens[None].astype(x.dtype), (B, N_META, D_MODEL))
    h_res = jnp.concatenate([meta, x], axis=1)
    L = h_res.shape[1]
    o_conv = 2 * CONV_CH
    o_q = o_conv + Q_W
    o_k = o_q + KV_W
    o_v = o_k + KV_W
    for i in range(DEPTH):
        h_res = h_res + 0.5 * swiglu(rms_norm(h_res, ffn1_norm[i]), ffn1_w_in[i], ffn1_w_out[i])
        h = rms_norm(h_res, mix_norm[i])
        proj = h @ w_in[i]
        y_a = conv_module(proj[..., :o_conv], conv_w[i], conv_b[i], conv_ln_g[i],
                          conv_ln_b[i], conv_w_out[i])
        q = rms_norm(proj[..., o_conv:o_q].reshape(B, L, N_Q_HEADS, HEAD_DIM), q_norm[i])
        k = rms_norm(proj[..., o_q:o_k].reshape(B, L, N_KV_HEADS, HEAD_DIM), k_norm[i])
        v = proj[..., o_k:o_v].reshape(B, L, N_KV_HEADS, HEAD_DIM)
        y_b = window_sink_attention(q, k, v, attn_sinks[i]) @ attn_w_out[i]
        gates = jax.nn.sigmoid(proj[..., o_v:] + gate_bias[i])
        merged = gates[..., :D_MODEL] * y_a + gates[..., D_MODEL:] * y_b
        h_res = h_res + merged @ w_out[i]
        h_res = h_res + 0.5 * swiglu(rms_norm(h_res, ffn2_norm[i]), ffn2_w_in[i], ffn2_w_out[i])
    return h_res[:, N_META:]


_drawn_inputs = setup_inputs


def setup_inputs(seed=0):
    import zlib

    import numpy as np

    out = dict(_drawn_inputs(seed))
    spreads = {}
    factors = {'gate_bias': 8.0,
     'conv_b': 3.191,
     'conv_ln_b': 6.589,
     'q_norm': 8.0,
     'k_norm': 8.0,
     'attn_sinks': 8.0}
    for name, (base, spread) in spreads.items():
        noise = np.random.default_rng([zlib.crc32(name.encode()), seed]).standard_normal(out[name].shape)
        drawn = base * np.exp(spread * noise) if base else spread * noise
        out[name] = __import__('jax').numpy.asarray(drawn.astype(out[name].dtype))
    for name, factor in factors.items():
        out[name] = (out[name] * factor).astype(out[name].dtype)
    return out
```

```python
from contextlib import ExitStack

import concourse.bass as bass
from concourse import mybir

F32, F32R = mybir.dt.float32, mybir.dt.float32r
ACT = mybir.ActivationFunctionType
ALU = mybir.AluOpType
AX = mybir.AxisListType

P = 128
DEPTH, D, SEQ, META = 2, 1024, 512, 16
CHUNK, HD, CONV_K = 64, 64, 31
FF = 2816
NT = META + SEQ
NH = NT // 2
KD, KF = D // P, FF // P
KB = KF // 2
NQ, NKV = D // HD, D // HD // 4
GROUPS = NKV
NCH = SEQ // CHUNK
PAD = CHUNK - META
WIN = 2 * CHUNK
KEYS = META + WIN
NEG = -1e30
EPS = 1e-6
O_B, O_Q = D, 2 * D
O_K = O_Q + NQ * HD
O_V = O_K + NKV * HD
O_GA = O_V + NKV * HD
O_GB = O_GA + D

R_FFN1, R_MIX, R_FFN2, R_CB, R_LG, R_LB, R_GA, R_GB, R_CW = range(9)
ROWS = R_CW + CONV_K

A, B, GA, GB = "a", "b", "ga", "gb"
FILL = [
    [(A, 0), (B, 0), (A, 1), (B, 1), (A, 2), (B, 2), (GA, 0), (GB, 0)],
    [(A, 3), (B, 3), (A, 4), (B, 4), (A, 5), (B, 5), (GA, 1), (GB, 1)],
    [(A, 6), (B, 6), (A, 7), (B, 7), (GA, 2), (GB, 2), (GA, 3), (GB, 3)],
    [(GA, 4), (GB, 4), (GA, 5), (GB, 5), (GA, 6), (GB, 6), (GA, 7), (GB, 7)],
]
PAR = 16 * (10 * DEPTH + 2 * DEPTH)
PRE = 2
GB_N = 11
TAPS = 7
U_SLOTS = 4

B_IN1, B_OUT1, B_MIX = 0, 2 * KF, 2 * KF + 2 * KD
B_ATT = B_MIX + GROUPS * GB_N
B_CONV, B_MO = B_ATT + KD, B_ATT + 2 * KD
B_IN2 = B_MO + KD
B_OUT2 = B_IN2 + 2 * KF
NBLK = B_OUT2 + 2 * KD
T_IN1, T_OUT1, T_MIX = 0, 2 * KF, 2 * KF + KD
T_ATT = T_MIX + GROUPS * GB_N
T_CONV, T_MO = T_ATT + KD, T_ATT + 2 * KD
T_IN2 = T_MO + KD
T_OUT2 = T_IN2 + 2 * KF
NOUT = T_OUT2 + KD

NPOS = 1 + NCH
SB = 3
NBAT = NPOS // SB


def tok0(pos):
    return 0 if pos == 0 else META + CHUNK * (pos - 1)


def npos(pos):
    return META if pos == 0 else CHUNK


def build(nc, x, meta_tokens, ffn1_norm, ffn1_w_in, ffn1_w_out, mix_norm, w_in, gate_bias, conv_w,
          conv_b, conv_ln_g, conv_ln_b, conv_w_out, q_norm, k_norm, attn_sinks, attn_w_out, w_out,
          ffn2_norm, ffn2_w_in, ffn2_w_out, out):
    rows = lambda w: w.rearrange("l (k p) n -> p l k n", p=P)
    ctx = ExitStack()
    with ctx:
        def sb(name, shape, dt=F32, at=ctx):
            return at.enter_context(nc.sbuf_tensor(name, shape, dt))

        def sem(name):
            return ctx.enter_context(nc.semaphore(name))

        resid = sb("resid", [P, KD, NT])
        xh, xl = sb("xh", [P, KD, NT], F32R), sb("xl", [P, KD, NT], F32R)
        raw = sb("raw", [P, 2, KB, P])
        wh, wl = sb("wh", [P, 2, KB, P], F32R), sb("wl", [P, 2, KB, P], F32R)
        rms = sb("rms", [P, NT])
        t0, t1 = sb("t0", [P, NT]), sb("t1", [P, NT])
        ident, ones = sb("ident", [P, P]), sb("ones", [P, P])
        prm = sb("prm", [P, KD, DEPTH * ROWS + 1])
        lp = sb("lp", [P, KD, ROWS])
        gnext = sb("gnext", [P, KD])
        qk = sb("qk", [HD, 4])
        gkq = sb("gkq", [HD, DEPTH])
        lgkq = sb("lgkq", [HD, 1])
        sink = sb("sink", [P, DEPTH, GROUPS, 2])
        lsink = sb("lsink", [P, GROUPS, 2])
        qrms = sb("qrms", [P, 2, NPOS])
        qstd = sb("qstd", [P, 2, NPOS])
        smax, negm = sb("smax", [P, 2, SB]), sb("negm", [P, 2, SB])
        sdif, sexp = sb("sdif", [P, 2, SB]), sb("sexp", [P, 2, SB])
        psum_p, rden = sb("psum_p", [P, 2, SB]), sb("rden", [P, 2, SB])
        eps1, eps64 = sb("eps1", [P, 1]), sb("eps64", [P, 1])

        load = ExitStack()
        xin = sb("xin", [P, 4, D], at=load)
        xmeta = sb("xmeta", [META, D], at=load)
        prow = sb("prow", [DEPTH * ROWS, D], at=load)
        qkrow = sb("qkrow", [4, HD], at=load)
        load.close()
        ffn = ExitStack()
        hh, hl = sb("hh", [P, KF, NT], F32R, ffn), sb("hl", [P, KF, NT], F32R, ffn)
        acc_f, sq_f = sb("acc_f", [P, NT], at=ffn), sb("sq_f", [P, NT], at=ffn)
        ffn.close()
        mix = ExitStack()
        ah, al = sb("ah", [P, KD, NT], F32R, mix), sb("al", [P, KD, NT], F32R, mix)
        cv = sb("cv", [P, KD, NT], at=mix)
        ub = sb("ub", [P, U_SLOTS, CONV_K - 1 + NT], at=mix)
        kvp = sb("kvp", [P, PAD + NT], at=mix)
        kn = sb("kn", [P, PAD + NT], at=mix)
        qb = sb("qb", [P, NT, 2], at=mix)
        vw = sb("vw", [P, NCH, HD], at=mix)
        vm = sb("vm", [META, HD], at=mix)
        pp = sb("pp", [P, 2, 2 * SB * KEYS], at=mix)
        pt = sb("pt", [P, 4, P], at=mix)
        gates_at = ExitStack()
        ga, gb = sb("ga", [P, KD, NT], at=gates_at), sb("gb", [P, KD, NT], at=gates_at)
        gates_at.close()
        mh, ml = sb("mh", [P, KD, NT], F32R, mix), sb("ml", [P, KD, NT], F32R, mix)
        mix.close()
        done = ExitStack()
        yout = sb("yout", [P, 4, D], at=done)
        done.close()
        acc_m, sq_m = pp[:, 0, 0:NT], pp[:, 1, 0:NT]
        qsq = pp[:, :, :].rearrange("p s n -> p (s n)")[:, 0:2 * NT].rearrange("p (n j) -> p n j", j=2)

        po = ctx.enter_context(nc.psum_tensor("po", [P, 4, 512], F32))
        pstat = ctx.enter_context(nc.psum_tensor("pstat", [P, 2, 512], F32))
        ptr = ctx.enter_context(nc.psum_tensor("ptr", [P, 512], F32))
        pov = ctx.enter_context(nc.psum_tensor("pov", [P, 512], F32))

        qss = [pstat[:, 0, NH:NH + NPOS], pov[:, 0:NPOS]]

        def slot(s):
            return po[:, 2 * s:2 * s + 2, 0:NH]

        def two(ap):
            return ap.rearrange("p (h n) -> p h n", h=2)

        def two1(ap):
            return ap.rearrange("p k (h n) -> p (k h) n", h=2)

        raw_in = [sem("raw_in0"), sem("raw_in1")]
        hi_done = sem("hi_done")
        lo_done = sem("lo_done")
        blk_used = sem("blk_used")
        out_taken = sem("out_taken")
        pre_in = sem("pre_in")
        par_in = sem("par_in")
        const_done = sem("const_done")
        pre_tr, pre_cp = sem("pre_tr"), sem("pre_cp")
        x_hi, x_sq, x_lo = sem("x_hi"), sem("x_sq"), sem("x_lo")
        acc_done = sem("acc_done")
        stat_ready, std_ready, rms_ready = sem("stat_ready"), sem("std_ready"), sem("rms_ready")
        silu_done, sr_done = sem("silu_done"), sem("sr_done")
        h_hi, h_lo = sem("h_hi"), sem("h_lo")
        lay = sem("lay")
        qsq_ready, ksq_ready = sem("qsq_ready"), sem("ksq_ready")
        qk_stat = sem("qk_stat")
        qstd_ready, kstd_ready, v_ready = sem("qstd_ready"), sem("kstd_ready"), sem("v_ready")
        qrms_ready, krms_ready, kn_ready = sem("qrms_ready"), sem("krms_ready"), sem("kn_ready")
        kn_dup = sem("kn_dup")
        tanh_done, u_ready = sem("tanh_done"), sem("u_ready")
        s_ready, sm_step, m_ready = sem("s_ready"), sem("sm_step"), sem("m_ready")
        exp_done, p_ready = sem("exp_done"), sem("p_ready")
        tr_ready, pt_ready, o_ready = sem("tr_ready"), sem("pt_ready"), sem("o_ready")
        pv_done = sem("pv_done")
        o_hi, o_lo = sem("o_hi"), sem("o_lo")
        conv_step = sem("conv_step")
        den_step, lay0 = sem("den_step"), sem("lay0")
        ln_acc, ln_mu, ln_d, ln_sq, ln_var = (sem(f"ln_{n}") for n in ("acc", "mu", "d", "sq", "var"))
        ln_std, ln_r, ln_y, ln_silu, ln_hi, ln_lo = (
            sem(f"ln_{n}") for n in ("std", "r", "y", "silu", "hi", "lo"))
        mg_b, mg_a, mg_sum, mg_hi, mg_lo = (sem(f"mg_{n}") for n in ("b", "a", "sum", "hi", "lo"))
        fin_tr, fin_cp, fin_out = sem("fin_tr"), sem("fin_cp"), sem("fin_out")

        block = ctx.enter_context(nc.Block())

        def blk(l, n):
            return l * NBLK + n

        def tile(l, n):
            return l * NOUT + n

        def norm(l, which):
            return l * 3 + which

        @block.sync
        def _(sp):
            for i in range(4):
                sp.dma_start(xin[:, i, :], x[0, i * P:(i + 1) * P, :]).then_inc(pre_in, 16)
            sp.dma_start(xmeta[:, :], meta_tokens).then_inc(pre_in, 16)
            for l in range(DEPTH):
                r = l * ROWS
                for row, src in ((R_FFN1, ffn1_norm), (R_MIX, mix_norm), (R_FFN2, ffn2_norm),
                                 (R_CB, conv_b), (R_LG, conv_ln_g), (R_LB, conv_ln_b)):
                    sp.dma_start(prow[r + row:r + row + 1, :], src[l:l + 1, :]).then_inc(par_in, 16)
                sp.dma_start(prow[r + R_GA:r + R_GA + 2, :],
                             gate_bias[l, :].rearrange("(a n) -> a n", a=2)).then_inc(par_in, 16)
                sp.dma_start(prow[r + R_CW:r + ROWS, :], conv_w[l, :, :]).then_inc(par_in, 16)
                sp.dma_start(qkrow[2 * l:2 * l + 1, :], q_norm[l:l + 1, :]).then_inc(par_in, 16)
                sp.dma_start(qkrow[2 * l + 1:2 * l + 2, :], k_norm[l:l + 1, :]).then_inc(par_in, 16)

            for l in range(DEPTH):
                for j in range(2):
                    src = attn_sinks[l, :].rearrange("(g j h) -> j g h", j=2, h=2)[j:j + 1, :, :]
                    sp.dma_start(sink[j::2, l, :, :],
                                 src.to_broadcast([HD, GROUPS, 2])).then_inc(par_in, 16)

            def load_block(l, n, s, halves):
                sp.wait_ge(lo_done, blk(l, n) + 1)
                for dst, src in halves:
                    sp.dma_start(dst, src).then_inc(raw_in[s], 16)

            def square(l, n, s, w, col):
                src = rows(w)
                load_block(l, n, s, [
                    (raw[:, s, k:k + 4, :],
                     src[:, bass.ds(l, 1), k:k + 4, bass.ds(col, P)].rearrange("p l k n -> p (l k) n"))
                    for k in (4, 0)])

            def ffn_loads(l, n_in, n_out, w_i, w_o):
                with sp.Fori(0, KF) as t:
                    square(l, n_in + 2 * t, 0, w_i, t * P)
                    square(l, n_in + 2 * t + 1, 1, w_i, t * P + FF)
                src = rows(w_o)
                with sp.Fori(0, KD) as m:
                    for s in range(2):
                        load_block(l, n_out + 2 * m + s, s, [
                            (raw[:, s, a:b, :],
                             src[:, bass.ds(l, 1), s * KB + a:s * KB + b, bass.ds(m * P, P)]
                             .rearrange("p l k n -> p (l k) n"))
                            for a, b in ((0, 6), (6, KB))])

            with sp.Fori(0, DEPTH) as l:
                ffn_loads(l, B_IN1, B_OUT1, ffn1_w_in, ffn1_w_out)
                src = rows(w_in)
                for g in range(GROUPS):
                    for i in range(GB_N):
                        n = B_MIX + g * GB_N + i
                        if i == 2:
                            load_block(l, n, n % 2, [
                                (raw[:, n % 2, 0:KD, a:a + HD],
                                 src[:, bass.ds(l, 1), :, c + HD * g:c + HD * g + HD]
                                 .rearrange("p l k n -> p (l k) n"))
                                for a, c in ((0, O_K), (HD, O_V))])
                        else:
                            if i < 2:
                                col = O_Q + (2 * g + i) * P
                            else:
                                kind, j = FILL[g][i - 3]
                                col = {A: 0, B: O_B, GA: O_GA, GB: O_GB}[kind] + j * P
                            square(l, n, n % 2, w_in, col)
                        if i == 7:
                            sp.wait_ge(kn_ready, l * GROUPS + g + 1)
                            sp.dma_start(kn[HD:P, PAD:], kn[0:HD, PAD:]).then_inc(kn_dup, 16)
                for n0, w in ((B_ATT, attn_w_out), (B_CONV, conv_w_out), (B_MO, w_out)):
                    with sp.Fori(0, KD // 2) as i:
                        for s in range(2):
                            square(l, n0 + 2 * i + s, s, w, i * 2 * P + s * P)
                ffn_loads(l, B_IN2, B_OUT2, ffn2_w_in, ffn2_w_out)

            for i in range(4):
                sp.wait_ge(fin_cp, i + 1)
                sp.dma_start(out[0, i * P:(i + 1) * P, :], yout[:, i, :]).then_inc(fin_out, 16)
            sp.wait_ge(fin_out, 64)

        @block.gpsimd
        def _(pool):
            nc.gpsimd.memset(ident[:, :], 0.0).then_inc(const_done, 1)
            nc.gpsimd.memset(ones[:, :], 1.0).then_inc(const_done, 1)
            pool.wait_ge(const_done, 2)
            nc.gpsimd.affine_select(out=ident[:, :], in_=ident[:, :], compare_op=ALU.not_equal, fill=1.0,
                                    base=0, pattern=[[-1, P]], channel_multiplier=1).then_inc(const_done, 1)
            nc.gpsimd.memset(eps1[:, :], EPS).then_inc(const_done, 1)
            nc.gpsimd.memset(eps64[:, :], HD * EPS).then_inc(lo_done, 2)

            def lo(l, n, s, k):
                pool.wait_ge(hi_done, blk(l, n) + 1)
                nc.gpsimd.tensor_tensor(wl[:, s, 0:k, :], raw[:, s, 0:k, :],
                                        wh[:, s, 0:k, :].bitcast(F32), ALU.subtract).then_inc(lo_done, 1)

            with pool.Fori(0, DEPTH) as l:
                for n0, count, k in ((B_IN1, 2 * KF, KD), (B_OUT1, 2 * KD, KB),
                                     (B_MIX, B_IN2 - B_MIX, KD),
                                     (B_IN2, 2 * KF, KD), (B_OUT2, 2 * KD, KB)):
                    with pool.Fori(0, count // 2) as i:
                        for s in range(2):
                            lo(l, n0 + 2 * i + s, s, k)

        @block.scalar
        def _(act):
            func = nc.scalar.activation

            def hi(l, half, s, k):
                pair = l * (NBLK // 2) + half
                act.wait_ge(raw_in[s], pair * 32 + 32)
                act.wait_ge(blk_used, pair * 2 + s + 1)
                func(wh[:, s, 0:k, :], raw[:, s, 0:k, :], ACT.Copy).then_inc(hi_done, 1)

            def x_parts(l, which, m, gain):
                act.wait_ge(acc_done, norm(l, which) * (KD + 1) + m + 1)
                xm = resid[:, bass.ds(m, 1), :].rearrange("p k n -> p (k n)")
                func(xh[:, bass.ds(m, 1), :].rearrange("p k n -> p (k n)"), xm, ACT.Identity,
                     scale=gain).then_inc(x_hi, 1)
                func(sq_of(which), xm, ACT.Square).then_inc(x_sq, 1)

            def sq_of(which):
                return sq_m if which == 2 else sq_f[:, :]

            def gain_of(row, m):
                if row is None:
                    return gnext[:, bass.ds(m, 1)]
                return lp[:, bass.ds(m, 1), row:row + 1].rearrange("p a b -> p (a b)")

            def std(l, which):
                act.wait_ge(stat_ready, norm(l, which) + 1)
                func(two(t0[:, :]), pstat[:, :, 0:NH], ACT.Sqrt, bias=eps1[:, :], scale=1.0 / D)\
                    .then_inc(std_ready, 1)

            def ffn_in(l, half, f, n_in, t_in, which, nxt):
                def step(t, first, last):
                    def hi_s(s):
                        hi(l, nxt[0] // 2 if last else half + t + 1, s, nxt[1] if last else KD)
                    hi_s(0)
                    if first:
                        std(l, which)
                    act.wait_ge(out_taken, tile(l, t_in) + 2 * t + 3)
                    func(t0[:, :], t0[:, :], ACT.Silu).then_inc(silu_done, 1)
                    hi_s(1)
                    act.wait_ge(out_taken, tile(l, t_in) + 2 * t + 4)
                    func(hh[:, bass.ds(t, 1), :].rearrange("p k n -> p (k n)"), t1[:, :], ACT.Copy)\
                        .then_inc(h_hi, 1)
                step(0, True, False)
                with act.Fori(1, KF - 1) as t:
                    step(t, False, False)
                step(KF - 1, False, True)

            def resid_out(l, half, t_out, which, row, nxt):
                lw, ww = (l, which) if which < 3 else (l + 1, 0)

                def step(m, last):
                    if not last:
                        for s in range(2):
                            hi(l, half + m + 1, s, KB)
                    elif nxt:
                        for s in range(2):
                            hi(l, nxt[0] // 2, s, nxt[1])
                    x_out(m)

                def x_out(m):
                    act.wait_ge(out_taken, tile(l, t_out) + m + 3)
                    x_parts(lw, ww, m, gain_of(row, m))
                return step, x_out

            act.wait_ge(const_done, 4)
            func(negm[:, 0, 0:1], eps1[:, :], ACT.Copy).then_inc(pt_ready, 1)
            for m in range(KD):
                act.wait_ge(pre_cp, PRE + m + 1)
                x_parts(0, 0, m, prm[:, m, R_FFN1:R_FFN1 + 1])

            def attn_exp(l, g, b):
                act.wait_ge(m_ready, (l * GROUPS + g) * NBAT + b + 1)
                for h in range(2):
                    for i in range(SB):
                        at = (h * SB + i) * KEYS
                        func(pp[:, (b + 1) % 2, at:at + KEYS], pstat[:, h, i * KEYS:(i + 1) * KEYS],
                             ACT.Exp, scale=qrms[:, h, b * SB + i:b * SB + i + 1],
                             bias=negm[:, h, i:i + 1], accum_out=psum_p[:, h, i:i + 1])
                func(sexp[:, :, :], sdif[:, :, :], ACT.Exp).then_inc(exp_done, 1)

            def take_pt(l, g, pos):
                n = (l * GROUPS + g) * NPOS + pos
                act.wait_ge(tr_ready, n + 1)
                act.wait_ge(pv_done, n + 1)
                flat = ptr[:, :].rearrange("p (a n) -> p a n", a=4)
                if pos:
                    func(pt[:, 0:2, :], flat[:, 0:2, :], ACT.Copy)
                func(pt[0:META, 2:4, :], flat[0:META, 2:4, :], ACT.Copy).then_inc(pt_ready, 1)

            def o_view(ap3, b):
                lo_, hi_ = tok0(b * SB), tok0(b * SB + SB - 1) + CHUNK
                return ap3[:, :, lo_:hi_], pov[:, 0:384].rearrange("p (j n) -> p j n", j=2)[:, :, 0:hi_ - lo_]

            def take_o(l, g, b):
                act.wait_ge(o_ready, (l * GROUPS + g) * NBAT + b + 1)
                dst, src = o_view(ah[:, 2 * g:2 * g + 2, :], b)
                func(dst, src, ACT.Copy).then_inc(o_hi, 1)

            def head_std(l, g):
                act.wait_ge(qk_stat, l * GROUPS + g + 1)
                for h in range(2):
                    ins = func(qstd[:, h, :], qss[h], ACT.Sqrt, bias=eps64[:, :])
                ins.then_inc(qstd_ready, 1)
                func(two(t0[0:HD, :]), pstat[0:HD, :, 0:NH], ACT.Sqrt, bias=eps1[0:HD, :],
                     scale=1.0 / HD).then_inc(kstd_ready, 1)
                func(vw[:, :, :], ptr[:, :].rearrange("p (c d) -> p c d", d=HD), ACT.Copy)
                func(vm[:, :], pov[0:META, 64:64 + HD], ACT.Copy).then_inc(v_ready, 1)

            def fill_tanh(l, g, i):
                kind, j = FILL[g][i - 3]
                if kind == A:
                    return
                act.wait_ge(out_taken, tile(l, T_MIX) + g * GB_N + i + 3)
                if kind == B:
                    func(t1[:, :], t1[:, :], ACT.Tanh, scale=0.5).then_inc(tanh_done, 1)
                else:
                    buf, row = (ga, R_GA) if kind == GA else (gb, R_GB)
                    func(buf[:, j, :], buf[:, j, :], ACT.Tanh, scale=0.5,
                         bias=lp[:, j, row:row + 1])

            def square_q(l, g, j):
                act.wait_ge(out_taken, tile(l, T_MIX) + g * GB_N + j + 3)
                func(qsq[:, :, j], qb[:, :, j], ACT.Square).then_inc(qsq_ready, 1)

            with act.Fori(0, DEPTH) as l:
                hi(l, 0, 0, KD)
                hi(l, 0, 1, KD)
                act.wait_ge(lay, l + 1)
                ffn_in(l, B_IN1 // 2, 0, B_IN1, T_IN1, 0, (B_OUT1, KB))
                step, _ = resid_out(l, B_OUT1 // 2, T_OUT1, 1, R_MIX, (B_MIX, KD))
                with act.Fori(0, KD - 1) as m:
                    step(m, False)
                step(KD - 1, True)

                for g in range(GROUPS):
                    def h(i):
                        n = B_MIX + g * GB_N + i + 2
                        hi(l, n // 2, n % 2, KD)
                    spill = g > 0
                    if spill:
                        take_pt(l, g - 1, 6)
                        take_pt(l, g - 1, 7)
                    h(0)
                    if g == 0:
                        std(l, 1)
                    if spill:
                        take_pt(l, g - 1, 8)
                    square_q(l, g, 0)
                    if spill:
                        take_o(l, g - 1, 2)
                    h(1)
                    square_q(l, g, 1)
                    h(2)
                    act.wait_ge(out_taken, tile(l, T_MIX) + g * GB_N + 2 + 3)
                    func(t0[0:HD, :], kvp[0:HD, PAD:], ACT.Square).then_inc(ksq_ready, 1)
                    h(3)
                    head_std(l, g)
                    fill_tanh(l, g, 3)
                    h(4)
                    fill_tanh(l, g, 4)
                    h(5)
                    fill_tanh(l, g, 5)
                    attn_exp(l, g, 0)
                    h(6)
                    fill_tanh(l, g, 6)
                    take_pt(l, g, 0)
                    h(7)
                    take_pt(l, g, 1)
                    fill_tanh(l, g, 7)
                    attn_exp(l, g, 1)
                    take_pt(l, g, 2)
                    h(8)
                    take_o(l, g, 0)
                    fill_tanh(l, g, 8)
                    take_pt(l, g, 3)
                    attn_exp(l, g, 2)
                    h(9)
                    take_pt(l, g, 4)
                    fill_tanh(l, g, 9)
                    take_pt(l, g, 5)
                    h(10)
                    take_o(l, g, 1)
                    fill_tanh(l, g, 10)
                g = GROUPS - 1
                for pos in (6, 7, 8):
                    take_pt(l, g, pos)
                take_o(l, g, 2)

                def block_hi(n):
                    hi(l, n // 2, n % 2, KD)
                for i in (2, 3, 4):
                    block_hi(B_ATT + i)
                for k in range(KD):
                    act.wait_ge(ln_d, l * KD + k + 1)
                    act.wait_ge(ln_acc, l * 2 * KD + KD + k)
                    func(sq_m, cv[:, k, :], ACT.Square).then_inc(ln_sq, 1)
                block_hi(B_ATT + 5)
                block_hi(B_ATT + 6)
                act.wait_ge(ln_var, l + 1)
                func(two(t0[:, :]), pstat[:, :, 0:NH], ACT.Sqrt, bias=eps1[:, :], scale=1.0 / D)\
                    .then_inc(ln_std, 1)
                for k in range(KD):
                    act.wait_ge(ln_y, l * KD + k + 1)
                    func(cv[:, k, :], cv[:, k, :], ACT.Silu, scale=lp[:, k, R_LG:R_LG + 1],
                         bias=lp[:, k, R_LB:R_LB + 1]).then_inc(ln_silu, 1)
                    act.wait_ge(ln_silu, l * KD + k + 1)
                    func(xh[:, k, :], cv[:, k, :], ACT.Copy).then_inc(ln_hi, 1)
                    if k in (1, 4, 7):
                        block_hi(B_ATT + {1: 7, 4: 8, 7: 9}[k])
                for m in range(KD):
                    block_hi(B_CONV + 2 + m)
                    act.wait_ge(mg_sum, l * KD + m + 1)
                    func(mh[:, m, :], t1[:, :], ACT.Copy).then_inc(mg_hi, 1)
                _, x_out = resid_out(l, 0, T_MO, 2, R_FFN2, None)
                with act.Fori(0, KD // 2) as i:
                    for s in range(2):
                        hi(l, (B_MO + 2) // 2 + i, s, KD)
                        x_out(2 * i + s)

                ffn_in(l, B_IN2 // 2, 1, B_IN2, T_IN2, 2, (B_OUT2, KB))
                step, _ = resid_out(l, B_OUT2 // 2, T_OUT2, 3, None, None)
                with act.Fori(0, KD - 1) as m:
                    step(m, False)
                step(KD - 1, True)

        @block.tensor
        def _(pe):
            mm, tr = nc.tensor.matmul, nc.tensor.transpose

            def products(l, n, s, out_slot, kt, mh_, ml_, first=True, last=True, before=None, mid=None):
                pe.wait_ge(lo_done, blk(l, n) + 3)
                for k in range(kt):
                    if before:
                        before(k)
                    if mid and k == kt // 2:
                        mid()
                    for w, v, end in ((wh, mh_, False), (wh, ml_, False), (wl, mh_, True)):
                        for h in range(2):
                            ins = mm(po[:, 2 * out_slot + h, 0:NH], w[:, s, k, :],
                                     v[:, k, h * NH:(h + 1) * NH],
                                     start=first and k == 0 and w is wh and v is mh_,
                                     stop=last and k == kt - 1 and end, skip_group_check=True)
                ins.then_inc(blk_used, 1)

            def free(l, t):
                pe.wait_ge(out_taken, tile(l, t) + 1)

            def stat(l, which):
                acc = acc_m if which == 2 else acc_f[:, :]
                pe.wait_ge(acc_done, (norm(l, which) + 1) * (KD + 1))
                for h in range(2):
                    ins = mm(pstat[:, h, 0:NH], ones[:, :], acc[:, h * NH:(h + 1) * NH], start=True, stop=True)
                ins.then_inc(stat_ready, 1)

            def x_tile(l, which):
                return lambda k: pe.wait_ge(x_lo, norm(l, which) * KD + k + 1)

            def ffn_in(l, n_in, t_in, which):
                def step(t, first):
                    free(l, t_in + 2 * t)
                    products(l, n_in + 2 * t, 0, 0, KD, xh, xl, before=x_tile(l, which) if first else None)
                    if first:
                        stat(l, which)
                    free(l, t_in + 2 * t + 1)
                    products(l, n_in + 2 * t + 1, 1, 1, KD, xh, xl)
                step(0, True)
                with pe.Fori(1, KF) as t:
                    step(t, False)

            def ffn_out(l, f, n_out, t_out):
                def step(i, first):
                    for j in range(2):
                        free(l, t_out + 2 * i + j)
                        for s in range(2):
                            if first and j == 0:
                                pe.wait_ge(h_lo, (l * 2 + f) * KF + KB * (s + 1))
                            products(l, n_out + 4 * i + 2 * j + s, s, j, KB,
                                     hh[:, s * KB:(s + 1) * KB, :], hl[:, s * KB:(s + 1) * KB, :],
                                     first=s == 0, last=s == 1)
                step(0, True)
                with pe.Fori(1, KD // 2) as i:
                    step(i, False)

            pe.wait_ge(const_done, 3)
            pe.wait_ge(par_in, PAR)
            nr = DEPTH * ROWS
            for k in range(KD):
                tr(pstat[:, k // 4, (k % 4) * nr:(k % 4 + 1) * nr], prow[:, k * P:(k + 1) * P],
                   ident[0:nr, 0:nr])
            tr(pov[0:HD, 0:4], qkrow[:, :], ident[0:4, 0:4]).then_inc(pre_tr, 1)
            pe.wait_ge(pre_in, 80)
            for k in range(KD):
                s = k % 2
                if k >= 2:
                    pe.wait_ge(pre_cp, PRE + k - 1)
                for i in range(4):
                    tr(po[:, 2 * s, i * P:(i + 1) * P], xin[:, i, k * P:(k + 1) * P], ident[:, :])
                tr(po[:, 2 * s + 1, 0:META], xmeta[:, k * P:(k + 1) * P],
                   ident[0:META, 0:META]).then_inc(pre_tr, 1)
            pe.wait_ge(pre_cp, PRE + KD)
            tr(ptr[:, 0:P], ident[:, :], ident[:, :]).then_inc(blk_used, 2)
            mm(ptr[:, 0:1], ident[:, :], ones[:, 0:1], start=True, stop=True).then_inc(pv_done, 1)

            def head_stats(l, g):
                pe.wait_ge(ksq_ready, l * GROUPS + g + 1)
                pe.wait_ge(qsq_ready, 2 * (l * GROUPS + g) + 2)
                pe.wait_ge(o_lo, (l * GROUPS + g) * NBAT + 1)
                for h in range(2):
                    for pos in range(NPOS):
                        mm(qss[h][:, pos:pos + 1], qsq[h * HD:(h + 1) * HD, tok0(pos):tok0(pos) + CHUNK, :].rearrange("p n j -> p (n j)"),
                           ones[h * HD:(h + 1) * HD, 0:1], start=True, stop=True)
                for h in range(2):
                    mm(pstat[0:HD, h, 0:NH], ones[0:HD, 0:HD], t0[0:HD, h * NH:(h + 1) * NH],
                       start=True, stop=True)
                for c in range(NCH):
                    tr(ptr[:, c * HD:(c + 1) * HD], kvp[HD:P, c * CHUNK:c * CHUNK + WIN], ident[HD:P, HD:P])
                tr(pov[0:META, 64:64 + HD], kvp[HD:P, PAD:PAD + META], ident[HD:P, HD:P]).then_inc(qk_stat, 1)

            def scores(l, g, b):
                n = (l * GROUPS + g) * NBAT + b
                if b == 0:
                    pe.wait_ge(kn_dup, 16 * (l * GROUPS + g + 1))
                else:
                    pe.wait_ge(exp_done, n)
                for h in range(2):
                    hs = slice(h * HD, (h + 1) * HD)
                    for i in range(SB):
                        pos = b * SB + i
                        q = qb[hs, tok0(pos):tok0(pos) + CHUNK, :].rearrange("p n j -> p (n j)")
                        ins = mm(pstat[:, h, i * KEYS:i * KEYS + META], q, kn[hs, PAD:PAD + META],
                                 start=True, stop=True)
                        if pos:
                            c = pos - 1
                            ins = mm(pstat[:, h, i * KEYS + META:(i + 1) * KEYS], q,
                                     kn[hs, c * CHUNK:c * CHUNK + WIN], start=True, stop=True)
                ins.then_inc(s_ready, 1)

            def turn(l, g, pos):
                n = (l * GROUPS + g) * NPOS + pos
                b, i = pos // SB, pos % SB
                pe.wait_ge(p_ready, (l * GROUPS + g) * NBAT + b + 1)
                pe.wait_ge(pt_ready, n + 1)
                for h in range(2):
                    at = (h * SB + i) * KEYS
                    if pos:
                        tr(ptr[:, h * P:(h + 1) * P], pp[:, (b + 1) % 2, at + META:at + KEYS], ident[:, :])
                    ins = tr(ptr[0:META, (2 + h) * P:(3 + h) * P], pp[:, (b + 1) % 2, at:at + META],
                             ident[:, :])
                ins.then_inc(tr_ready, 1)

            def mix_values(l, g, pos):
                n = (l * GROUPS + g) * NPOS + pos
                b = pos // SB
                pe.wait_ge(pt_ready, n + 2)
                if pos % SB == 0:
                    pe.wait_ge(o_lo, (l * GROUPS + g) * NBAT + b + 1)
                w, off = npos(pos), tok0(pos) - tok0(b * SB)
                for h in range(2):
                    dst = pov[h * HD:(h + 1) * HD, 0:384].rearrange("p (j n) -> p j n", j=2)[:, :, off:off + w]
                    cut = lambda a: a.rearrange("p (n j) -> p j n", j=2)[:, :, 0:w]
                    if pos:
                        mm(dst, vw[:, pos - 1, :], cut(pt[:, h, :]), start=True, stop=False,
                           skip_group_check=True)
                    ins = mm(dst, vm[:, :], cut(pt[0:META, 2 + h, :]), start=pos == 0, stop=True,
                             skip_group_check=True)
                ins.then_inc(pv_done, 1)
                if pos % SB == SB - 1:
                    mm(pov[0:1, 511:512], ones[:, 0:1], ones[:, 0:1], start=True, stop=True)\
                        .then_inc(o_ready, 1)

            def mixer_in(l):
                for g in range(GROUPS):
                    T = lambda pos, gg=g: turn(l, gg, pos)
                    V = lambda pos, gg=g: mix_values(l, gg, pos)
                    S = lambda b, gg=g: scores(l, gg, b)
                    before = g - 1

                    def do(*steps):
                        return lambda: [f() for f in steps]
                    mids = {7: do(lambda: S(1), lambda: T(0)), 8: do(lambda: V(1), lambda: T(2)),
                            9: do(lambda: T(3)), 10: do(lambda: V(4), lambda: T(5))}
                    ends = {3: do(lambda: head_stats(l, g)), 5: do(lambda: S(0)),
                            7: do(lambda: V(0), lambda: T(1)), 8: do(lambda: V(2), lambda: S(2)),
                            9: do(lambda: V(3), lambda: T(4)), 10: do(lambda: V(5), lambda: T(6))}
                    if g:
                        mids[0] = do(lambda: V(6, before), lambda: T(7, before))
                        ends[0] = do(lambda: V(7, before), lambda: T(8, before))
                        mids[1] = do(lambda: V(8, before))
                    else:
                        mids[0] = do(lambda: stat(l, 1))
                    for i in range(GB_N):
                        n = g * GB_N + i
                        free(l, T_MIX + n)
                        products(l, B_MIX + n, n % 2, n % 2, KD, xh, xl, mid=mids.get(i),
                                 before=x_tile(l, 1) if n == 0 else None)
                        if i in ends:
                            ends[i]()
                for pos in (6, 7, 8):
                    mix_values(l, GROUPS - 1, pos)
                    if pos < 8:
                        turn(l, GROUPS - 1, pos + 1)

            with pe.Fori(0, DEPTH) as l:
                ffn_in(l, B_IN1, T_IN1, 0)
                ffn_out(l, 0, B_OUT1, T_OUT1)
                mixer_in(l)
                for m in range(KD):
                    free(l, T_ATT + m)
                    if m == 0:
                        pe.wait_ge(o_lo, (l + 1) * GROUPS * NBAT + 1)
                    products(l, B_ATT + m, m % 2, m % 2, KD, ah, al)
                    if m == 2:
                        pe.wait_ge(ln_acc, l * 2 * KD + KD - 1)
                        for h in range(2):
                            ins = mm(pstat[:, h, 0:NH], ones[:, :], acc_m[:, h * NH:(h + 1) * NH],
                                     start=True, stop=True)
                        ins.then_inc(ln_mu, 1)
                    if m == 4:
                        pe.wait_ge(ln_acc, (l + 1) * 2 * KD)
                        for h in range(2):
                            ins = mm(pstat[:, h, 0:NH], ones[:, :], acc_m[:, h * NH:(h + 1) * NH],
                                     start=True, stop=True)
                        ins.then_inc(ln_var, 1)
                for m in range(KD):
                    free(l, T_CONV + m)
                    products(l, B_CONV + m, m % 2, m % 2, KD, xh, xl,
                             before=(lambda k: pe.wait_ge(ln_lo, l * KD + k + 1)) if m == 0 else None)
                for m in range(KD):
                    free(l, T_MO + m)
                    products(l, B_MO + m, m % 2, m % 2, KD, mh, ml,
                             before=(lambda k: pe.wait_ge(mg_lo, l * KD + k + 1)) if m == 0 else None)
                ffn_in(l, B_IN2, T_IN2, 2)
                ffn_out(l, 1, B_OUT2, T_OUT2)

            pe.wait_ge(out_taken, DEPTH * NOUT + 2)
            for i in range(4):
                s = i % 2
                if i >= 2:
                    pe.wait_ge(fin_cp, i - 1)
                for k in range(KD):
                    ins = tr(po[:, 2 * s + k // 4, (k % 4) * P:(k % 4 + 1) * P],
                             resid[:, k, META + i * P:META + (i + 1) * P], ident[:, :])
                ins.then_inc(fin_tr, 1)

        @block.vector
        def _(dve):
            tt, ts, stt = nc.vector.tensor_tensor, nc.vector.tensor_scalar, nc.vector.scalar_tensor_tensor
            flat = lambda ap: ap.rearrange("p k n -> p (k n)")

            def at(ap, m):
                return flat(ap[:, bass.ds(m, 1), :])

            dve.wait_ge(pre_tr, 1)
            nc.vector.memset(prm[:, :, DEPTH * ROWS:], 0.0)
            nc.vector.tensor_copy(prm[:, :, 0:DEPTH * ROWS].rearrange("p (a k) r -> p a k r", a=2),
                                  pstat[:, :, 0:4 * DEPTH * ROWS].rearrange("p a (k r) -> p a k r", k=4))\
                .then_inc(pre_cp, 1)
            nc.vector.tensor_copy(qk[:, :], pov[0:HD, 0:4]).then_inc(pre_cp, 1)
            dve.wait_ge(pre_cp, 2)
            qkv = qk[:, :].rearrange("p (l a) -> p l a", a=2)
            tt(gkq[:, :], qkv[:, :, 0], qkv[:, :, 1], ALU.mult)
            nc.vector.memset(acc_f[:, :], 0.0).then_inc(acc_done, 1)
            for k in range(KD):
                s = k % 2
                dve.wait_ge(pre_tr, 2 + k)
                nc.vector.tensor_copy(resid[:, k, META:], po[:, 2 * s, 0:512])
                nc.vector.tensor_copy(resid[:, k, 0:META], po[:, 2 * s + 1, 0:META]).then_inc(pre_cp, 1)

            def x_lo_part(l, which, m, gain):
                n = norm(l, which)
                sq, acc = (sq_m, acc_m) if which == 2 else (sq_f[:, :], acc_f[:, :])
                dve.wait_ge(x_hi, n * KD + m + 1)
                stt(at(xl, m), at(resid, m), gain, at(xh, m).bitcast(F32),
                    ALU.mult, ALU.subtract).then_inc(x_lo, 1)
                dve.wait_ge(x_sq, n * KD + m + 1)
                dve.wait_ge(acc_done, n * (KD + 1) + m + 1)
                tt(acc, acc, sq, ALU.add).then_inc(acc_done, 1)

            for k in range(KD):
                x_lo_part(0, 0, k, prm[:, k, R_FFN1:R_FFN1 + 1])
            nc.vector.memset(sdif[:, :, :], 0.0).then_inc(out_taken, 2)
            nc.vector.memset(smax[:, :, :], 0.0).then_inc(o_lo, 1)

            def ready(l, n):
                dve.wait_ge(blk_used, blk(l, n) + 3)

            def rms_of(l, which):
                dve.wait_ge(std_ready, norm(l, which) + 1)
                nc.vector.reciprocal(rms[:, :], t0[:, :]).then_inc(rms_ready, 1)

            def ffn_in(l, f, n_in, t_in, which):
                rms_of(l, which)

                def step(t):
                    n = (l * 2 + f) * KF + t
                    dve.wait_ge(rms_ready, norm(l, which) + 1)
                    ready(l, n_in + 2 * t)
                    tt(two(t0[:, :]), slot(0), two(rms[:, :]), ALU.mult).then_inc(out_taken, 1)
                    dve.wait_ge(silu_done, n + 1)
                    tt(t0[:, :], t0[:, :], rms[:, :], ALU.mult).then_inc(sr_done, 1)
                    ready(l, n_in + 2 * t + 1)
                    dve.wait_ge(sr_done, n + 1)
                    tt(two(t1[:, :]), slot(1), two(t0[:, :]), ALU.mult).then_inc(out_taken, 1)
                    dve.wait_ge(h_hi, n + 1)
                    tt(at(hl, t), t1[:, :], at(hh, t).bitcast(F32), ALU.subtract).then_inc(h_lo, 1)
                with dve.Fori(0, KF) as t:
                    step(t)

            def resid_out(l, n_out, per, t_out, which, row):
                lw, ww = (l, which) if which < 3 else (l + 1, 0)
                acc = acc_m if ww == 2 else acc_f[:, :]
                nc.vector.memset(acc, 0.0).then_inc(acc_done, 1)
                with dve.Fori(0, KD // 2) as i:
                    for s in range(2):
                        m = 2 * i + s
                        ready(l, n_out + per * m + per - 1)
                        stt(two(at(resid, m)), slot(s), 0.5, two(at(resid, m)), ALU.mult, ALU.add)\
                            .then_inc(out_taken, 1)
                        gain = gnext[:, bass.ds(m, 1)] if row is None else flat(
                            lp[:, bass.ds(m, 1), row:row + 1])
                        x_lo_part(lw, ww, m, gain)

            def taps(l, first, last):
                for n in range(first, last):
                    pair, r = divmod(n, 2 * CONV_K)
                    j, k = 2 * pair + r % 2, r // 2
                    u = ub[:, j % U_SLOTS, k:k + NT]
                    w = lp[:, j, R_CW + k:R_CW + k + 1]
                    if k == 0:
                        dve.wait_ge(u_ready, l * KD + j + 1)
                        ts(cv[:, j, :], u, w, lp[:, j, R_CB:R_CB + 1], ALU.mult, ALU.add).then_inc(conv_step, 1)
                    else:
                        dve.wait_ge(conv_step, l * KD * CONV_K + n - 1)
                        stt(cv[:, j, :], u, w, cv[:, j, :], ALU.mult, ALU.add).then_inc(conv_step, 1)

            def take(l, g, i):
                n = g * GB_N + i
                ready(l, B_MIX + n)
                if i < 2:
                    dst = qb[:, :, i]
                elif i == 2:
                    dst = kvp[:, PAD:]
                else:
                    kind, j = FILL[g][i - 3]
                    if kind == A:
                        if j >= U_SLOTS:
                            dve.wait_ge(conv_step, l * KD * CONV_K + ((j - U_SLOTS) // 2 + 1) * 2 * CONV_K)
                        stt(two(ub[:, j % U_SLOTS, CONV_K - 1:]), slot(n % 2), 0.5, two(rms[:, :]),
                            ALU.mult, ALU.mult).then_inc(out_taken, 1)
                        return
                    dst = t1[:, :] if kind == B else (ga if kind == GA else gb)[:, j, :]
                tt(two(dst), slot(n % 2), two(rms[:, :]), ALU.mult).then_inc(out_taken, 1)

            def glu(l, g, i):
                if i < 3 or FILL[g][i - 3][0] != B:
                    return
                j = FILL[g][i - 3][1]
                dve.wait_ge(tanh_done, l * KD + j + 1)
                u = ub[:, j % U_SLOTS, CONV_K - 1:]
                stt(u, t1[:, :], 1.0, u, ALU.add, ALU.mult).then_inc(u_ready, 1)

            def head_rms(l, g):
                n = l * GROUPS + g
                dve.wait_ge(qstd_ready, n + 1)
                nc.vector.reciprocal(qrms[:, :, :], qstd[:, :, :]).then_inc(qrms_ready, 1)
                dve.wait_ge(kstd_ready, n + 1)
                nc.vector.reciprocal(t0[0:HD, :], t0[0:HD, :]).then_inc(krms_ready, 1)
                dve.wait_ge(krms_ready, n + 1)
                stt(kn[0:HD, PAD:], kvp[0:HD, PAD:], lgkq[:, :], t0[0:HD, :], ALU.mult, ALU.mult)\
                    .then_inc(kn_ready, 1)

            steps = 5

            def row_max(l, g, b):
                n = (l * GROUPS + g) * NBAT + b
                dve.wait_ge(s_ready, n + 1)
                s3 = pstat[:, :, 0:SB * KEYS].rearrange("p h (i k) -> p h i k", i=SB)
                if b == 0:
                    nc.vector.memset(s3[:, :, 0, META:], NEG)
                    nc.vector.memset(s3[:, :, 1, META:META + CHUNK], NEG)
                nc.vector.memset(negm[:, :, :], 0.0).then_inc(sm_step, 1)
                dve.wait_ge(sm_step, n * steps + 1)
                nc.vector.tensor_reduce(smax[:, :, :], s3, AX.X, ALU.max).then_inc(sm_step, 1)
                dve.wait_ge(sm_step, n * steps + 2)
                q = qrms[:, :, b * SB:(b + 1) * SB]
                tt(smax[:, :, :], smax[:, :, :], q, ALU.mult).then_inc(sm_step, 1)
                dve.wait_ge(sm_step, n * steps + 3)
                sk = lsink[:, g, :].rearrange("p (h o) -> p h o", o=1).to_broadcast([P, 2, SB])
                tt(smax[:, :, :], smax[:, :, :], sk, ALU.max).then_inc(sm_step, 1)
                dve.wait_ge(sm_step, n * steps + 4)
                ts(negm[:, :, :], smax[:, :, :], -1.0, None, ALU.mult).then_inc(sm_step, 1)
                tt(sdif[:, :, :], sk, smax[:, :, :], ALU.subtract).then_inc(m_ready, 1)

            def norm_p(l, g, b):
                n = (l * GROUPS + g) * NBAT + b
                dve.wait_ge(exp_done, n + 1)
                tt(rden[:, :, :], psum_p[:, :, :], sexp[:, :, :], ALU.add).then_inc(den_step, 1)
                dve.wait_ge(den_step, 2 * n + 1)
                nc.vector.reciprocal(rden[:, :, :], rden[:, :, :]).then_inc(den_step, 1)
                dve.wait_ge(den_step, 2 * n + 2)
                p3 = pp[:, (b + 1) % 2, :].rearrange("p (t k) -> p t k", k=KEYS)
                rd = rden[:, :, :].rearrange("p h (i o) -> p (h i) o", o=1).to_broadcast([P, 2 * SB, KEYS])
                tt(p3, p3, rd, ALU.mult).then_inc(p_ready, 1)

            def o_lo_part(l, g, b):
                dve.wait_ge(o_hi, (l * GROUPS + g) * NBAT + b + 1)
                a, z = tok0(b * SB), tok0(b * SB + SB - 1) + CHUNK
                src = pov[:, 0:384].rearrange("p (j n) -> p j n", j=2)[:, :, 0:z - a]
                js = slice(2 * g, 2 * g + 2)
                tt(al[:, js, a:z], src, ah[:, js, a:z].bitcast(F32), ALU.subtract).then_inc(o_lo, 1)

            with dve.Fori(0, DEPTH) as l:
                dve.wait_ge(x_sq, norm(l, 0) * KD + KD)
                dve.wait_ge(x_lo, norm(l, 0) * KD + KD)
                prl = prm[:, :, bass.ds(l * ROWS, ROWS)]
                nc.vector.tensor_copy(lp[:, :, :], prl)
                nc.vector.tensor_copy(gnext[:, :], prm[:, :, bass.ds(l * ROWS + ROWS, 1)].rearrange(
                    "p k o -> p (k o)"))
                nc.vector.tensor_copy(lgkq[:, :], gkq[:, bass.ds(l, 1)])
                dve.wait_ge(par_in, PAR)
                nc.vector.tensor_copy(lsink[:, :, :], sink[:, bass.ds(l, 1), :, :].rearrange(
                    "p l g h -> p (l g) h")).then_inc(lay0, 1)
                dve.wait_ge(lay0, l + 1)
                ts(lp[:, :, R_GA:R_GB + 1], lp[:, :, R_GA:R_GB + 1], 0.5, None, ALU.mult).then_inc(lay, 1)
                dve.wait_ge(lay, l + 1)

                ffn_in(l, 0, B_IN1, T_IN1, 0)
                resid_out(l, B_OUT1, 2, T_OUT1, 1, R_MIX)

                nc.vector.memset(ub[:, :, 0:CONV_K - 1], 0.0)
                nc.vector.memset(kvp[:, 0:PAD], 0.0)
                nc.vector.memset(kn[:, 0:PAD], 0.0)
                rms_of(l, 1)
                dve.wait_ge(rms_ready, norm(l, 1) + 1)
                tap = 0
                for g in range(GROUPS):
                    for i in range(GB_N):
                        take(l, g, i)
                        if i == 1 and g:
                            o_lo_part(l, g - 1, 2)
                        if i == 3:
                            head_rms(l, g)
                        if i == 5:
                            row_max(l, g, 0)
                        if i == 6:
                            norm_p(l, g, 0)
                        if i == 7:
                            row_max(l, g, 1)
                        if i == 8:
                            norm_p(l, g, 1)
                            row_max(l, g, 2)
                            o_lo_part(l, g, 0)
                        if i == 10:
                            o_lo_part(l, g, 1)
                        if (g, i) > (0, 6):
                            n = min(tap + TAPS, KD * CONV_K)
                            taps(l, tap, n)
                            tap = n
                        glu(l, g, i)
                        if i == 9:
                            norm_p(l, g, 2)
                o_lo_part(l, GROUPS - 1, 2)

                def take_att(m):
                    ready(l, B_ATT + m)
                    stt(two(gb[:, m, :]), two(gb[:, m, :]), 1.0, slot(m % 2), ALU.add, ALU.mult)\
                        .then_inc(out_taken, 1)
                taps(l, tap, KD * CONV_K)
                dve.wait_ge(conv_step, (l + 1) * KD * CONV_K)
                n = l * 2 * KD
                tt(acc_m, cv[:, 0, :], cv[:, 1, :], ALU.add).then_inc(ln_acc, 1)
                for k in range(2, KD):
                    dve.wait_ge(ln_acc, n + k - 1)
                    tt(acc_m, acc_m, cv[:, k, :], ALU.add).then_inc(ln_acc, 1)
                take_att(0)
                take_att(1)
                take_att(2)
                dve.wait_ge(ln_mu, l + 1)
                nc.vector.memset(acc_m, 0.0).then_inc(ln_acc, 1)
                for k in range(KD + 1):
                    if k < KD:
                        stt(two(cv[:, k, :]), pstat[:, :, 0:NH], -1.0 / D, two(cv[:, k, :]), ALU.mult,
                            ALU.add).then_inc(ln_d, 1)
                    if k:
                        dve.wait_ge(ln_sq, l * KD + k)
                        dve.wait_ge(ln_acc, n + KD + k - 1)
                        tt(acc_m, acc_m, sq_m, ALU.add).then_inc(ln_acc, 1)
                take_att(3)
                take_att(4)
                dve.wait_ge(ln_std, l + 1)
                nc.vector.reciprocal(rms[:, :], t0[:, :]).then_inc(ln_r, 1)
                dve.wait_ge(ln_r, l + 1)
                take_att(5)
                for k in range(KD + 1):
                    if k < KD:
                        tt(cv[:, k, :], cv[:, k, :], rms[:, :], ALU.mult).then_inc(ln_y, 1)
                    if k:
                        dve.wait_ge(ln_hi, l * KD + k)
                        tt(xl[:, k - 1, :], cv[:, k - 1, :], xh[:, k - 1, :].bitcast(F32), ALU.subtract)\
                            .then_inc(ln_lo, 1)
                    if k == 4:
                        take_att(6)
                take_att(7)
                for m in range(KD):
                    ready(l, B_CONV + m)
                    if m:
                        dve.wait_ge(mg_lo, l * KD + m)
                    stt(two(t1[:, :]), two(ga[:, m, :]), 1.0, slot(m % 2), ALU.add, ALU.mult)\
                        .then_inc(out_taken, 1)
                    dve.wait_ge(out_taken, tile(l, T_CONV) + m + 3)
                    tt(t1[:, :], t1[:, :], gb[:, m, :], ALU.add).then_inc(mg_sum, 1)
                    dve.wait_ge(mg_hi, l * KD + m + 1)
                    tt(ml[:, m, :], t1[:, :], mh[:, m, :].bitcast(F32), ALU.subtract).then_inc(mg_lo, 1)
                resid_out(l, B_MO, 1, T_MO, 2, R_FFN2)
                ffn_in(l, 1, B_IN2, T_IN2, 2)
                resid_out(l, B_OUT2, 2, T_OUT2, 3, None)

            for i in range(4):
                dve.wait_ge(fin_tr, i + 1)
                nc.vector.tensor_copy(yout[:, i, :].rearrange("p (a n) -> p a n", a=2),
                                      po[:, 2 * (i % 2):2 * (i % 2) + 2, :]).then_inc(fin_cp, 1)


_INS = ["x", "meta_tokens", "ffn1_norm", "ffn1_w_in", "ffn1_w_out", "mix_norm", "w_in", "gate_bias",
        "conv_w", "conv_b", "conv_ln_g", "conv_ln_b", "conv_w_out", "q_norm", "k_norm", "attn_sinks",
        "attn_w_out", "w_out", "ffn2_norm", "ffn2_w_in", "ffn2_w_out"]


def kernel(**inputs):
    import numpy as np
    import concourse.bacc as bacc
    from concourse.bass_utils import run_bass_kernel_spmd

    nc = bacc.Bacc("TRN2", target_bir_lowering=False, num_devices=1)
    arrays, args = {}, []
    for name in _INS:
        a = np.ascontiguousarray(inputs[name])
        arrays[f"in_{name}"] = a
        args.append(nc.dram_tensor(f"in_{name}", a.shape, mybir.dt.from_np(a.dtype), kind="ExternalInput").ap())
    out = nc.dram_tensor("out_0", (1, SEQ, D), F32, kind="ExternalOutput").ap()
    build(nc, *args, out)
    r = run_bass_kernel_spmd(nc, [arrays], core_ids=[0])
    return r.results[0]["out_0"]
```

```python
from contextlib import ExitStack

import concourse.bass as bass
from concourse import mybir

F32, F32R = mybir.dt.float32, mybir.dt.float32r
ACT = mybir.ActivationFunctionType
ALU = mybir.AluOpType
AX = mybir.AxisListType

P = 128
DEPTH, D, SEQ, META = 2, 1024, 512, 16
CHUNK, HD, CONV_K = 64, 64, 31
FF = 2816
NT = META + SEQ
NH = NT // 2
KD, KF = D // P, FF // P
KB = KF // 2
NQ, NKV = D // HD, D // HD // 4
GROUPS = NKV
NCH = SEQ // CHUNK
PAD = CHUNK - META
WIN = 2 * CHUNK
NEG = -1e30
EPS = 1e-6
O_B, O_Q = D, 2 * D
O_K = O_Q + NQ * HD
O_V = O_K + NKV * HD
O_GA = O_V + NKV * HD
O_GB = O_GA + D

R_FFN1, R_MIX, R_FFN2, R_CB, R_LG, R_LB, R_GA, R_GB, R_CW = range(9)
ROWS = R_CW + CONV_K
TB_GATE, TB_CONV = R_GA * DEPTH, R_CW * DEPTH

A, B, GA, GB = "a", "b", "ga", "gb"
FILL = [
    [(A, 0), (B, 0), (A, 1), (B, 1), (A, 2), (B, 2), (A, 3), (B, 3)],
    [(GA, 0), (GB, 0), (GA, 1), (GB, 1), (A, 4), (B, 4), (A, 5), (B, 5)],
    [(GA, 2), (GB, 2), (GA, 3), (GB, 3), (A, 6), (B, 6), (A, 7), (B, 7)],
    [(GA, 4), (GB, 4), (GA, 5), (GB, 5), (GA, 6), (GB, 6), (GA, 7), (GB, 7)],
]
CONSTS = 4
PAR, PAR_SINK = 16 * 10, 16 * 2
PRE = 2
GB_N = 11
TAPS = (9, 8, 7, 6, 7, 8, 3, 7, 4, 5, 8)
LATE = 9
U_SLOTS = 4
LN_SUMS = 2 * KD - 1

B_IN1, B_OUT1, B_MIX = 0, 2 * KF, 2 * KF + 2 * KD
B_ATT = B_MIX + GROUPS * GB_N
B_CONV, B_MO = B_ATT + KD, B_ATT + 2 * KD
B_IN2 = B_MO + KD
B_OUT2 = B_IN2 + 2 * KF
NBLK = B_OUT2 + 2 * KD
T_IN1, T_OUT1, T_MIX = 0, 2 * KF, 2 * KF + KD
T_ATT = T_MIX + GROUPS * GB_N
T_CONV, T_MO = T_ATT + KD, T_ATT + 2 * KD
T_IN2 = T_MO + KD
T_OUT2 = T_IN2 + 2 * KF
NOUT = T_OUT2 + KD

NPOS = 1 + NCH
SB = 3
NBAT = NPOS // SB
WK = WIN + META
NS = 2 * SB * WK
PW = max(NS, 3 * NT // 2)
MB = 2 * META


def tap_order():
    order, active, left = [], [0], {j: 0 for j in range(KD)}
    nxt = 1
    while active:
        for j in list(active):
            order.append((j, left[j]))
            left[j] += 1
            if left[j] == CONV_K:
                active.remove(j)
        if nxt < KD and (len(order) >= TAPS[5] + TAPS[6] if nxt == 1 else len(active) < 2):
            active.append(nxt)
            nxt += 1
    return order


ORDER = tap_order()
STEP_OF = {tap: n + 1 for n, tap in enumerate(ORDER)}


def tok0(pos):
    return 0 if pos == 0 else META + CHUNK * (pos - 1)


def npos(pos):
    return META if pos == 0 else CHUNK


def build(nc, x, meta_tokens, ffn1_norm, ffn1_w_in, ffn1_w_out, mix_norm, w_in, gate_bias, conv_w,
          conv_b, conv_ln_g, conv_ln_b, conv_w_out, q_norm, k_norm, attn_sinks, attn_w_out, w_out,
          ffn2_norm, ffn2_w_in, ffn2_w_out, out):
    rows = lambda w: w.rearrange("l (k p) n -> p l k n", p=P)
    ctx = ExitStack()
    with ctx:
        def sb(name, shape, dt=F32, at=ctx):
            return at.enter_context(nc.sbuf_tensor(name, shape, dt))

        def sem(name):
            return ctx.enter_context(nc.semaphore(name))

        resid = sb("resid", [P, KD, NT])
        xh, xl = sb("xh", [P, KD, NT], F32R), sb("xl", [P, KD, NT], F32R)
        raw = sb("raw", [P, 2, KB, P])
        wh, wl = sb("wh", [P, 2, KB, P], F32R), sb("wl", [P, 2, KB, P], F32R)
        rms = sb("rms", [P, NT])
        t0, t1 = sb("t0", [P, NT]), sb("t1", [P, NT])
        ident, ones = sb("ident", [P, P]), sb("ones", [P, P])
        prm = sb("prm", [P, KD, DEPTH * ROWS])
        lp = sb("lp", [P, KD, ROWS])
        gnext = sb("gnext", [P, KD])
        qk = sb("qk", [HD, 4])
        gkq = sb("gkq", [HD, DEPTH])
        lgkq = sb("lgkq", [HD, 1])
        sink = sb("sink", [P, DEPTH, GROUPS, 2])
        lsink = sb("lsink", [P, GROUPS, 2])
        qstd = sb("qstd", [P, NPOS, 2])
        qrms, nqrms = sb("qrms", [P, NPOS, 2]), sb("nqrms", [P, NPOS, 2])
        smax, negm = sb("smax", [P, SB, 2]), sb("negm", [P, SB, 2])
        sdif, sexp = sb("sdif", [P, SB, 2]), sb("sexp", [P, SB, 2])
        psum, rden = sb("psum", [P, SB, 2]), sb("rden", [P, SB, 2])
        eps1, eps64, halves = sb("eps1", [P, 1]), sb("eps64", [P, 1]), sb("halves", [P, 2])

        load = ExitStack()
        xin = sb("xin", [P, 4, D], at=load)
        xmeta = sb("xmeta", [META, D], at=load)
        prow = sb("prow", [DEPTH * ROWS, D], at=load)
        qkrow = sb("qkrow", [4, HD], at=load)
        load.close()
        ffn = ExitStack()
        hh, hl = sb("hh", [P, KF, NT], F32R, ffn), sb("hl", [P, KF, NT], F32R, ffn)
        acc_f, sq_f = sb("acc_f", [P, NT], at=ffn), sb("sq_f", [P, 2, NT], at=ffn)
        ffn.close()
        mix = ExitStack()
        ah, al = sb("ah", [P, KD, NT], F32R, mix), sb("al", [P, KD, NT], F32R, mix)
        cv = sb("cv", [P, KD, NT], at=mix)
        ub = sb("ub", [P, U_SLOTS, CONV_K - 1 + NT], at=mix)
        kvp = sb("kvp", [P, PAD + NT], at=mix)
        kn = sb("kn", [P, 2, PAD + NT], at=mix)
        qb = sb("qb", [P, NT, 2], at=mix)
        vw = sb("vw", [P, NCH, HD], at=mix)
        vm = sb("vm", [MB, P], at=mix)
        pw = sb("pw", [P, 2, PW], at=mix)
        pt = sb("pt", [P, 2, P], at=mix)
        ptm = sb("ptm", [MB, P], at=mix)
        gates_at = ExitStack()
        ga, gb = sb("ga", [P, KD, NT], at=gates_at), sb("gb", [P, KD, NT], at=gates_at)
        gates_at.close()
        mh, ml = sb("mh", [P, KD, NT], F32R, mix), sb("ml", [P, KD, NT], F32R, mix)
        mix.close()
        done = ExitStack()
        yout = sb("yout", [P, 4, D], at=done)
        done.close()
        pflat = pw[:, :, :].rearrange("p s n -> p (s n)")
        acc_m, sq_m = pflat[:, 0:NT], pflat[:, NT:3 * NT].rearrange("p (s n) -> p s n", s=2)
        qsq = pflat[:, 0:2 * NT].rearrange("p (n j) -> p n j", j=2)

        po = ctx.enter_context(nc.psum_tensor("po", [P, 4, 512], F32))
        pstat = ctx.enter_context(nc.psum_tensor("pstat", [P, 2, 512], F32))
        ptr = ctx.enter_context(nc.psum_tensor("ptr", [P, 512], F32))
        pov = ctx.enter_context(nc.psum_tensor("pov", [P, 512], F32))

        qss = pov[:, 0:2 * NPOS].rearrange("p (n h) -> p n h", h=2)
        sflat = pstat[:, :, :].rearrange("p b n -> p (b n)")
        scr = pstat[:, :, 0:SB * WK].rearrange("p b (r k) -> p b r k", k=WK)

        def score_col(i, h):
            return (2 * i + h) // SB * 512 + (2 * i + h) % SB * WK

        def s_win(i):
            a, step = score_col(i, 0), score_col(i, 1) + META - score_col(i, 0)
            return sflat[:, a:a + 2 * step].rearrange("p (h n) -> p h n", h=2)[:, :, 0:WIN]

        def slot(s):
            return po[:, 2 * s:2 * s + 2, 0:NH]

        def two(ap):
            return ap.rearrange("p (h n) -> p h n", h=2)

        def two1(ap):
            return ap.rearrange("p k (h n) -> p (k h) n", h=2)

        raw_in = [sem("raw_in0"), sem("raw_in1")]
        hi_done = sem("hi_done")
        lo_done = sem("lo_done")
        blk_used = sem("blk_used")
        out_taken = sem("out_taken")
        pre_in = sem("pre_in")
        par_in, sink_in = sem("par_in"), sem("sink_in")
        const_done, halves_done = sem("const_done"), sem("halves_done")
        pre_tr, pre_cp = sem("pre_tr"), sem("pre_cp")
        x_hi, x_sq, x_lo = sem("x_hi"), sem("x_sq"), sem("x_lo")
        acc_done = sem("acc_done")
        stat_ready, std_ready, rms_ready = sem("stat_ready"), sem("std_ready"), sem("rms_ready")
        silu_done, sr_done = sem("silu_done"), sem("sr_done")
        h_hi, h_lo = sem("h_hi"), sem("h_lo")
        lay = sem("lay")
        qsq_ready, ksq_ready = sem("qsq_ready"), sem("ksq_ready")
        qk_stat = sem("qk_stat")
        qstd_ready, kstd_ready, v_ready = sem("qstd_ready"), sem("kstd_ready"), sem("v_ready")
        qrms_ready, krms_ready, kn_ready = sem("qrms_ready"), sem("krms_ready"), sem("kn_ready")
        kn_dup = sem("kn_dup")
        tanh_done, u_ready = sem("tanh_done"), sem("u_ready")
        s_ready, mask_done, m_ready = sem("s_ready"), sem("mask_done"), sem("m_ready")
        max_step, neg_step = sem("max_step"), sem("neg_step")
        exp_done, p_ready = sem("exp_done"), sem("p_ready")
        tr_ready, pt_ready, pv_done = sem("tr_ready"), sem("pt_ready"), sem("pv_done")
        o_hi, o_lo = sem("o_hi"), sem("o_lo")
        conv_step = sem("conv_step")
        den_step, lay0 = sem("den_step"), sem("lay0")
        ln_acc, ln_mu, ln_d, ln_sq, ln_var = (sem(f"ln_{n}") for n in ("acc", "mu", "d", "sq", "var"))
        ln_std, ln_r, ln_y, ln_silu, ln_hi, ln_lo = (
            sem(f"ln_{n}") for n in ("std", "r", "y", "silu", "hi", "lo"))
        mg_sum, mg_hi, mg_lo = (sem(f"mg_{n}") for n in ("sum", "hi", "lo"))
        fin_tr, fin_cp, fin_out = sem("fin_tr"), sem("fin_cp"), sem("fin_out")

        block = ctx.enter_context(nc.Block())

        def blk(l, n):
            return l * NBLK + n

        def tile(l, n):
            return l * NOUT + n

        def norm(l, which):
            return l * 3 + which

        @block.sync
        def _(sp):
            for i in range(4):
                sp.dma_start(xin[:, i, :], x[0, i * P:(i + 1) * P, :]).then_inc(pre_in, 16)
            sp.dma_start(xmeta[:, :], meta_tokens).then_inc(pre_in, 16)
            def load_block(l, n, s, halves):
                sp.wait_ge(lo_done, blk(l, n) + 1)
                for dst, src in halves:
                    sp.dma_start(dst, src).then_inc(raw_in[s], 16)

            def square(l, n, s, w, col, layer=None):
                src = rows(w)
                layer = l if layer is None else layer
                load_block(l, n, s, [
                    (raw[:, s, k:k + 4, :],
                     src[:, bass.ds(layer, 1), k:k + 4, bass.ds(col, P)].rearrange("p l k n -> p (l k) n"))
                    for k in (4, 0)])

            def ffn_pair(l, layer, n_in, w_i, t):
                square(l, n_in + 2 * t, 0, w_i, t * P, layer)
                square(l, n_in + 2 * t + 1, 1, w_i, t * P + FF, layer)

            def ffn_loads(l, n_in, n_out, w_i, w_o, start):
                with sp.Fori(start, KF) as t:
                    ffn_pair(l, l, n_in, w_i, t)
                src = rows(w_o)
                with sp.Fori(0, KD) as m:
                    for s in range(2):
                        load_block(l, n_out + 2 * m + s, s, [
                            (raw[:, s, a:b, :],
                             src[:, bass.ds(l, 1), s * KB + a:s * KB + b, bass.ds(m * P, P)]
                             .rearrange("p l k n -> p (l k) n"))
                            for a, b in ((0, 6), (6, KB))])

            ffn_pair(0, 0, B_IN1, ffn1_w_in, 0)
            with sp.Fori(0, DEPTH) as l:
                ffn_loads(l, B_IN1, B_OUT1, ffn1_w_in, ffn1_w_out, 1)
                src = rows(w_in)
                for g in range(GROUPS):
                    for i in range(GB_N):
                        n = B_MIX + g * GB_N + i
                        if i == 2:
                            load_block(l, n, n % 2, [
                                (raw[:, n % 2, 0:KD, a:a + HD],
                                 src[:, bass.ds(l, 1), :, c + HD * g:c + HD * g + HD]
                                 .rearrange("p l k n -> p (l k) n"))
                                for a, c in ((0, O_K), (HD, O_V))])
                        else:
                            if i < 2:
                                col = O_Q + (2 * g + i) * P
                            else:
                                kind, j = FILL[g][i - 3]
                                col = {A: 0, B: O_B, GA: O_GA, GB: O_GB}[kind] + j * P
                            square(l, n, n % 2, w_in, col)
                        if i == 7:
                            sp.wait_ge(kn_ready, l * GROUPS + g + 1)
                            sp.dma_start(kn[HD:P, 1, PAD:], kn[0:HD, 0, PAD:]).then_inc(kn_dup, 16)
                for n0, w in ((B_ATT, attn_w_out), (B_CONV, conv_w_out), (B_MO, w_out)):
                    with sp.Fori(0, KD // 2) as i:
                        for s in range(2):
                            square(l, n0 + 2 * i + s, s, w, i * 2 * P + s * P)
                ffn_loads(l, B_IN2, B_OUT2, ffn2_w_in, ffn2_w_out, 0)
                ffn_pair(l + 1, DEPTH - 1, B_IN1, ffn1_w_in, 0)

            for i in range(4):
                sp.wait_ge(fin_cp, i + 1)
                sp.dma_start(out[0, i * P:(i + 1) * P, :], yout[:, i, :]).then_inc(fin_out, 16)
            sp.wait_ge(fin_out, 64)

        @block.gpsimd
        def _(pool):
            nc.gpsimd.memset(eps64[:, :], HD * EPS).then_inc(lo_done, 2)
            nc.gpsimd.memset(ident[:, :], 0.0).then_inc(const_done, 1)
            nc.gpsimd.memset(ones[:, :], 1.0).then_inc(const_done, 1)
            nc.gpsimd.memset(eps1[:, :], EPS).then_inc(const_done, 1)
            pool.wait_ge(const_done, 3)
            nc.gpsimd.affine_select(out=ident[:, :], in_=ident[:, :], compare_op=ALU.not_equal, fill=1.0,
                                    base=0, pattern=[[-1, P]], channel_multiplier=1).then_inc(const_done, 1)

            def lo(l, n, s, k):
                pool.wait_ge(hi_done, blk(l, n) + 1)
                nc.gpsimd.tensor_tensor(wl[:, s, 0:k, :], raw[:, s, 0:k, :],
                                        wh[:, s, 0:k, :].bitcast(F32), ALU.subtract).then_inc(lo_done, 1)

            with pool.Fori(0, DEPTH) as l:
                for n0, count, k in ((B_IN1, 2 * KF, KD), (B_OUT1, 2 * KD, KB),
                                     (B_MIX, B_IN2 - B_MIX, KD),
                                     (B_IN2, 2 * KF, KD), (B_OUT2, 2 * KD, KB)):
                    with pool.Fori(0, count // 2) as i:
                        for s in range(2):
                            lo(l, n0 + 2 * i + s, s, k)
            for s in range(2):
                lo(DEPTH, s, s, KD)

        @block.scalar
        def _(act):
            func = nc.scalar.activation
            for row, src in ((R_FFN1, ffn1_norm), (R_MIX, mix_norm), (R_FFN2, ffn2_norm),
                             (R_CB, conv_b), (R_LG, conv_ln_g), (R_LB, conv_ln_b)):
                act.dma_start(prow[row * DEPTH:(row + 1) * DEPTH, :], src).then_inc(par_in, 16)
            act.dma_start(prow[TB_GATE:TB_CONV, :], gate_bias.rearrange("l (a n) -> (l a) n", a=2))\
                .then_inc(par_in, 16)
            act.dma_start(prow[TB_CONV:, :], conv_w.rearrange("l k n -> (l k) n")).then_inc(par_in, 16)
            act.dma_start(qkrow[0:DEPTH, :], q_norm).then_inc(par_in, 16)
            act.dma_start(qkrow[DEPTH:, :], k_norm).then_inc(par_in, 16)
            for j in range(2):
                src = attn_sinks.rearrange("l (g j h) -> j l g h", j=2, h=2)[j:j + 1, :, :, :]
                act.dma_start(sink[j::2, :, :, :], src.to_broadcast([HD, DEPTH, GROUPS, 2]))\
                    .then_inc(sink_in, 16)

            def hi(l, half, s, k):
                pair = l * (NBLK // 2) + half
                act.wait_ge(raw_in[s], pair * 32 + 32)
                act.wait_ge(blk_used, pair * 2 + s + 1)
                func(wh[:, s, 0:k, :], raw[:, s, 0:k, :], ACT.Copy).then_inc(hi_done, 1)

            def x_parts(l, which, m, s, gain):
                act.wait_ge(acc_done, norm(l, which) * (KD + 2) + m + 1)
                xm = resid[:, bass.ds(m, 1), :].rearrange("p k n -> p (k n)")
                func(xh[:, bass.ds(m, 1), :].rearrange("p k n -> p (k n)"), xm, ACT.Identity,
                     scale=gain).then_inc(x_hi, 1)
                func(sq_of(which)[:, s, :], xm, ACT.Square).then_inc(x_sq, 1)

            def sq_of(which):
                return sq_m if which == 2 else sq_f[:, :, :]

            def gain_of(row, m):
                if row is None:
                    return gnext[:, bass.ds(m, 1)]
                return lp[:, bass.ds(m, 1), row:row + 1].rearrange("p a b -> p (a b)")

            def std(l, which):
                act.wait_ge(stat_ready, norm(l, which) + 1)
                func(two(t0[:, :]), pstat[:, :, 0:NH], ACT.Sqrt, bias=eps1[:, :], scale=1.0 / D)\
                    .then_inc(std_ready, 1)

            def ffn_in(l, half, f, n_in, t_in, which, nxt):
                def step(t, first, last):
                    def hi_s(s):
                        hi(l, nxt[0] // 2 if last else half + t + 1, s, nxt[1] if last else KD)
                    if first:
                        std(l, which)
                    hi_s(0)
                    act.wait_ge(out_taken, tile(l, t_in) + 2 * t + 3)
                    func(t0[:, :], t0[:, :], ACT.Silu).then_inc(silu_done, 1)
                    hi_s(1)
                    act.wait_ge(out_taken, tile(l, t_in) + 2 * t + 4)
                    func(hh[:, bass.ds(t, 1), :].rearrange("p k n -> p (k n)"), t1[:, :], ACT.Copy)\
                        .then_inc(h_hi, 1)
                step(0, True, False)
                with act.Fori(1, KF - 1) as t:
                    step(t, False, False)
                step(KF - 1, False, True)

            def resid_out(l, half, t_out, which, row, nxt):
                lw, ww = (l, which) if which < 3 else (l + 1, 0)

                def step(i, last):
                    for j in range(2):
                        m = 2 * i + j
                        for s in range(2):
                            if last and j:
                                hi(l, nxt[0] // 2, s, nxt[1])
                            else:
                                hi(l, half + m + 1, s, KB)
                        x_out(m, j)

                def x_out(m, j):
                    act.wait_ge(out_taken, tile(l, t_out) + m + 3)
                    x_parts(lw, ww, m, j, gain_of(row, m))
                return step, x_out

            act.wait_ge(const_done, CONSTS)
            func(negm[:, 0, 0:1], eps1[:, :], ACT.Copy).then_inc(pt_ready, 1)
            for m in range(KD):
                act.wait_ge(pre_cp, PRE + m + 1)
                x_parts(0, 0, m, m % 2, prm[:, m, R_FFN1 * DEPTH:R_FFN1 * DEPTH + 1])
                if m < 2:
                    hi(0, 0, m, KD)

            def attn_exp(l, g, b, i):
                if i == 0:
                    act.wait_ge(m_ready, (l * GROUPS + g) * NBAT + b + 1)
                for h in range(2):
                    scale, bias = qrms[:, b * SB + i, h:h + 1], negm[:, i, h:h + 1]
                    at = (2 * i + h) * WK
                    func(pw[:, (b + 1) % 2, at:at + WK], sflat[:, score_col(i, h):score_col(i, h) + WK],
                         ACT.Exp, scale=scale, bias=bias, accum_out=psum[:, i, h:h + 1])
                if i == SB - 1:
                    func(sexp[:, :, :], sdif[:, :, :], ACT.Exp).then_inc(exp_done, 1)

            def take_pt(l, g, pos):
                n = (l * GROUPS + g) * NPOS + pos
                act.wait_ge(tr_ready, n + 1)
                act.wait_ge(pv_done, n + 1)
                if pos:
                    func(pt[:, :, :], ptr[:, 0:2 * P].rearrange("p (h n) -> p h n", h=2), ACT.Copy)
                func(ptm[:, :], ptr[0:MB, 2 * P:3 * P], ACT.Copy).then_inc(pt_ready, 1)

            def o_view(ap3, b):
                lo_, hi_ = tok0(b * SB), tok0(b * SB + SB - 1) + CHUNK
                return ap3[:, :, lo_:hi_], pov[:, 0:384].rearrange("p (j n) -> p j n", j=2)[:, :, 0:hi_ - lo_]

            def take_o(l, g, b):
                act.wait_ge(pv_done, (l * GROUPS + g) * NPOS + (b + 1) * SB + 1)
                dst, src = o_view(ah[:, 2 * g:2 * g + 2, :], b)
                func(dst, src, ACT.Copy).then_inc(o_hi, 1)

            def head_std(l, g):
                act.wait_ge(qk_stat, l * GROUPS + g + 1)
                func(qstd[:, :, :], qss, ACT.Sqrt, bias=eps64[:, :]).then_inc(qstd_ready, 1)
                func(two(t0[0:HD, :]), pstat[0:HD, :, 0:NH], ACT.Sqrt, bias=eps1[0:HD, :],
                     scale=1.0 / HD).then_inc(kstd_ready, 1)
                func(vw[:, :, :], ptr[:, :].rearrange("p (c d) -> p c d", d=HD), ACT.Copy)
                func(vm[0:META, 0:HD], pov[0:META, 64:64 + HD], ACT.Copy)
                func(vm[:, HD:P], pov[0:MB, 128:128 + HD], ACT.Copy).then_inc(v_ready, 1)

            def fill_tanh(l, g, i):
                kind, j = FILL[g][i - 3]
                if kind == A:
                    return
                act.wait_ge(out_taken, tile(l, T_MIX) + g * GB_N + i + 3)
                if kind == B:
                    func(t1[:, :], t1[:, :], ACT.Tanh, scale=0.5).then_inc(tanh_done, 1)
                else:
                    buf, row = (ga, R_GA) if kind == GA else (gb, R_GB)
                    func(buf[:, j, :], buf[:, j, :], ACT.Tanh, scale=0.5,
                         bias=lp[:, j, row:row + 1])

            def square_q(l, g, j):
                act.wait_ge(out_taken, tile(l, T_MIX) + g * GB_N + j + 3)
                func(qsq[:, :, j], qb[:, :, j], ACT.Square).then_inc(qsq_ready, 1)

            with act.Fori(0, DEPTH) as l:
                act.wait_ge(lay, l + 1)
                ffn_in(l, B_IN1 // 2, 0, B_IN1, T_IN1, 0, (B_OUT1, KB))
                step, _ = resid_out(l, B_OUT1 // 2, T_OUT1, 1, R_MIX, (B_MIX, KD))
                with act.Fori(0, KD // 2 - 1) as i:
                    step(i, False)
                step(KD // 2 - 1, True)

                for g in range(GROUPS):
                    def h(i):
                        n = B_MIX + g * GB_N + i + 2
                        hi(l, n // 2, n % 2, KD)
                    spill = g > 0
                    if spill:
                        take_pt(l, g - 1, 6)
                        take_pt(l, g - 1, 7)
                    if g == 0:
                        std(l, 1)
                    h(0)
                    if spill:
                        take_pt(l, g - 1, 8)
                    square_q(l, g, 0)
                    if spill:
                        take_o(l, g - 1, 2)
                    h(1)
                    square_q(l, g, 1)
                    h(2)
                    act.wait_ge(out_taken, tile(l, T_MIX) + g * GB_N + 2 + 3)
                    func(t0[0:HD, :], kvp[0:HD, PAD:], ACT.Square).then_inc(ksq_ready, 1)
                    h(3)
                    head_std(l, g)
                    fill_tanh(l, g, 3)
                    h(4)
                    fill_tanh(l, g, 4)
                    h(5)
                    fill_tanh(l, g, 5)
                    for i in range(SB):
                        attn_exp(l, g, 0, i)
                    h(6)
                    fill_tanh(l, g, 6)
                    h(7)
                    take_pt(l, g, 0)
                    fill_tanh(l, g, 7)
                    attn_exp(l, g, 1, 0)
                    take_pt(l, g, 1)
                    attn_exp(l, g, 1, 1)
                    attn_exp(l, g, 1, 2)
                    h(8)
                    take_pt(l, g, 2)
                    fill_tanh(l, g, 8)
                    attn_exp(l, g, 2, 0)
                    attn_exp(l, g, 2, 1)
                    take_o(l, g, 0)
                    take_pt(l, g, 3)
                    attn_exp(l, g, 2, 2)
                    h(9)
                    take_pt(l, g, 4)
                    fill_tanh(l, g, 9)
                    take_pt(l, g, 5)
                    h(10)
                    take_o(l, g, 1)
                    fill_tanh(l, g, 10)
                g = GROUPS - 1
                for pos in (6, 7, 8):
                    take_pt(l, g, pos)
                take_o(l, g, 2)

                def block_hi(n):
                    hi(l, n // 2, n % 2, KD)
                block_hi(B_ATT + 2)
                block_hi(B_ATT + 3)
                for k in range(KD):
                    act.wait_ge(ln_d, l * KD + k + 1)
                    act.wait_ge(ln_acc, l * LN_SUMS + KD - 1 + max(k - 1, 0))
                    func(sq_m[:, k % 2, :], cv[:, k, :], ACT.Square).then_inc(ln_sq, 1)
                    if k == 4:
                        block_hi(B_ATT + 4)
                block_hi(B_ATT + 5)
                act.wait_ge(ln_var, l + 1)
                func(two(t0[:, :]), pstat[:, :, 0:NH], ACT.Sqrt, bias=eps1[:, :], scale=1.0 / D)\
                    .then_inc(ln_std, 1)
                block_hi(B_ATT + 6)
                for k in range(KD):
                    act.wait_ge(ln_y, l * KD + k + 1)
                    func(cv[:, k, :], cv[:, k, :], ACT.Silu, scale=lp[:, k, R_LG:R_LG + 1],
                         bias=lp[:, k, R_LB:R_LB + 1]).then_inc(ln_silu, 1)
                    act.wait_ge(ln_silu, l * KD + k + 1)
                    func(xh[:, k, :], cv[:, k, :], ACT.Copy).then_inc(ln_hi, 1)
                    if k in (2, 6):
                        block_hi(B_ATT + (7 if k == 2 else 8))
                block_hi(B_ATT + 9)
                for m in range(KD):
                    block_hi(B_CONV + 2 + m)
                    act.wait_ge(mg_sum, l * KD + m + 1)
                    func(mh[:, m, :], t1[:, :], ACT.Copy).then_inc(mg_hi, 1)
                _, x_out = resid_out(l, 0, T_MO, 2, R_FFN2, None)
                with act.Fori(0, KD // 2) as i:
                    for s in range(2):
                        hi(l, (B_MO + 2) // 2 + i, s, KD)
                        x_out(2 * i + s, s)

                ffn_in(l, B_IN2 // 2, 1, B_IN2, T_IN2, 2, (B_OUT2, KB))
                step, _ = resid_out(l, B_OUT2 // 2, T_OUT2, 3, None, (NBLK, KD))
                with act.Fori(0, KD // 2 - 1) as i:
                    step(i, False)
                step(KD // 2 - 1, True)

        @block.tensor
        def _(pe):
            mm, tr = nc.tensor.matmul, nc.tensor.transpose

            def products(l, n, s, out_slot, kt, mh_, ml_, first=True, last=True, before=None, mid=None,
                         k0=0, done=True):
                pe.wait_ge(lo_done, blk(l, n) + 3)
                for k in range(k0, kt):
                    if before:
                        before(k)
                    if mid and k == (kt - 2 if before else kt // 2):
                        mid()
                    for w, v, end in ((wh, mh_, False), (wh, ml_, False), (wl, mh_, True)):
                        for h in range(2):
                            ins = mm(po[:, 2 * out_slot + h, 0:NH], w[:, s, k, :],
                                     v[:, k, h * NH:(h + 1) * NH],
                                     start=first and k == 0 and w is wh and v is mh_,
                                     stop=last and k == kt - 1 and end, skip_group_check=True)
                if done:
                    ins.then_inc(blk_used, 1)

            def free(l, t):
                pe.wait_ge(out_taken, tile(l, t) + 1)

            def stat(l, which):
                acc = acc_m if which == 2 else acc_f[:, :]
                pe.wait_ge(acc_done, (norm(l, which) + 1) * (KD + 2))
                for h in range(2):
                    ins = mm(pstat[:, h, 0:NH], ones[:, :], acc[:, h * NH:(h + 1) * NH], start=True, stop=True)
                ins.then_inc(stat_ready, 1)

            def x_tile(l, which):
                return lambda k: pe.wait_ge(x_lo, norm(l, which) * KD + k + 1)

            def ffn_in(l, n_in, t_in, which):
                def step(t, first):
                    free(l, t_in + 2 * t)
                    products(l, n_in + 2 * t, 0, 0, KD, xh, xl, before=x_tile(l, which) if first else None,
                             mid=(lambda: stat(l, which)) if first else None)
                    free(l, t_in + 2 * t + 1)
                    products(l, n_in + 2 * t + 1, 1, 1, KD, xh, xl)
                step(0, True)
                with pe.Fori(1, KF) as t:
                    step(t, False)

            def ffn_out(l, f, n_out, t_out):
                def step(i, first):
                    for j in range(2):
                        free(l, t_out + 2 * i + j)
                        for s in range(2):
                            if first and j == 0:
                                pe.wait_ge(h_lo, (l * 2 + f) * KF + KB * (s + 1))
                            products(l, n_out + 4 * i + 2 * j + s, s, j, KB,
                                     hh[:, s * KB:(s + 1) * KB, :], hl[:, s * KB:(s + 1) * KB, :],
                                     first=s == 0, last=s == 1)
                step(0, True)
                with pe.Fori(1, KD // 2) as i:
                    step(i, False)

            pe.wait_ge(const_done, CONSTS)
            pe.wait_ge(halves_done, 4)
            tr(ptr[:, 0:P], ident[:, :], ident[:, :]).then_inc(blk_used, 2)
            mm(ptr[:, 0:1], ident[:, :], ones[:, 0:1], start=True, stop=True).then_inc(pv_done, 1)
            pe.wait_ge(par_in, PAR)
            nr = DEPTH * ROWS
            for k in range(KD):
                tr(pstat[:, k // 4, (k % 4) * nr:(k % 4 + 1) * nr], prow[:, k * P:(k + 1) * P],
                   ident[0:nr, 0:nr])
            tr(pov[0:HD, 0:2 * DEPTH], qkrow[:, :], ident[0:4, 0:4]).then_inc(pre_tr, 1)
            pe.wait_ge(pre_in, 80)
            for k in range(KD):
                s = k % 2
                if k >= 2:
                    pe.wait_ge(pre_cp, PRE + k - 1)
                for i in range(4):
                    tr(po[:, 2 * s, i * P:(i + 1) * P], xin[:, i, k * P:(k + 1) * P], ident[:, :])
                tr(po[:, 2 * s + 1, 0:META], xmeta[:, k * P:(k + 1) * P],
                   ident[0:META, 0:META]).then_inc(pre_tr, 1)
            pe.wait_ge(pre_cp, PRE + KD)

            def head_stats(l, g):
                pe.wait_ge(ksq_ready, l * GROUPS + g + 1)
                pe.wait_ge(qsq_ready, 2 * (l * GROUPS + g) + 2)
                pe.wait_ge(o_lo, (l * GROUPS + g) * NBAT + 1)
                for pos in range(NPOS):
                    mm(qss[:, pos, :], qsq[:, tok0(pos):tok0(pos) + CHUNK, :].rearrange("p n j -> p (n j)"),
                       halves[:, :], start=True, stop=True)
                for h in range(2):
                    mm(pstat[0:HD, h, 0:NH], ones[0:HD, 0:HD], t0[0:HD, h * NH:(h + 1) * NH],
                       start=True, stop=True)
                for c in range(NCH):
                    tr(ptr[:, c * HD:(c + 1) * HD], kvp[HD:P, c * CHUNK:c * CHUNK + WIN], ident[HD:P, HD:P])
                tr(pov[0:META, 64:64 + HD], kvp[HD:P, PAD:PAD + META], ident[HD:P, HD:P])
                tr(pov[0:MB, 128:128 + HD], kvp[HD:P, PAD + META - MB:PAD + META], ident[HD:P, HD:P])\
                    .then_inc(qk_stat, 1)

            def scores(l, g, b):
                n = (l * GROUPS + g) * NBAT + b
                if b == 0:
                    pe.wait_ge(kn_dup, 16 * (l * GROUPS + g + 1))
                else:
                    pe.wait_ge(exp_done, n)

                for i in range(SB):
                    pos = b * SB + i
                    q = qb[:, tok0(pos):tok0(pos) + CHUNK, :].rearrange("p n j -> p (n j)")
                    if pos:
                        c = pos - 1
                        win = kn[:, :, c * CHUNK:c * CHUNK + WIN]
                        if i == SB // 2:
                            for h in range(2):
                                mm(s_win(i)[:, h, :], q, win[:, h, :], start=True, stop=True)
                        else:
                            mm(s_win(i), q, win, start=True, stop=True)
                    meta = kn[:, :, PAD:PAD + META]
                    if i == SB // 2:
                        mm(sflat[:, score_col(i, 0) + WIN:score_col(i, 0) + WK], q, meta[:, 0, :],
                           start=True, stop=True)
                        ins = mm(sflat[:, score_col(i, 1):score_col(i, 1) + META], q, meta[:, 1, :],
                                 start=True, stop=True)
                    else:
                        ins = mm(sflat[:, score_col(i, 0) + WIN:score_col(i, 1) + META]
                                 .rearrange("p (h n) -> p h n", h=2), q, meta, start=True, stop=True)
                ins.then_inc(s_ready, 1)

            def turn(l, g, pos):
                n = (l * GROUPS + g) * NPOS + pos
                b, i = pos // SB, pos % SB
                pe.wait_ge(p_ready, (l * GROUPS + g) * NBAT + b + 1)
                pe.wait_ge(pt_ready, n + 1)
                if pos:
                    for h in range(2):
                        at = (2 * i + h) * WK + h * META
                        tr(ptr[:, h * P:(h + 1) * P], pw[:, (b + 1) % 2, at:at + WIN], ident[:, :])
                at = 2 * i * WK + WIN
                tr(ptr[0:MB, 2 * P:3 * P], pw[:, (b + 1) % 2, at:at + MB], ident[:, :])\
                    .then_inc(tr_ready, 1)

            def mix_values(l, g, pos):
                n = (l * GROUPS + g) * NPOS + pos
                b = pos // SB
                pe.wait_ge(pt_ready, n + 2)
                if pos % SB == 0:
                    pe.wait_ge(o_lo, (l * GROUPS + g) * NBAT + b + 1)
                w, off = npos(pos), tok0(pos) - tok0(b * SB)
                dst = pov[:, 0:384].rearrange("p (j n) -> p j n", j=2)[:, :, off:off + w]
                cut = lambda a: a.rearrange("p (n j) -> p j n", j=2)[:, :, 0:w]
                if pos:
                    for h in range(2):
                        mm(dst[h * HD:(h + 1) * HD], vw[:, pos - 1, :], cut(pt[:, h, :]), start=True,
                           stop=False, skip_group_check=True)
                mm(dst, vm[:, :], cut(ptm[:, :]), start=pos == 0, stop=True,
                   skip_group_check=True).then_inc(pv_done, 1)

            def mixer_in(l):
                for g in range(GROUPS):
                    T = lambda pos, gg=g: turn(l, gg, pos)
                    V = lambda pos, gg=g: mix_values(l, gg, pos)
                    S = lambda b, gg=g: scores(l, gg, b)
                    before = g - 1

                    def do(*steps):
                        return lambda: [f() for f in steps]
                    mids = {7: do(lambda: S(1)), 8: do(lambda: V(0), lambda: T(1)),
                            9: do(lambda: V(2), lambda: T(3)), 10: do(lambda: V(4), lambda: T(5))}
                    ends = {3: do(lambda: head_stats(l, g)), 5: do(lambda: S(0)), 7: do(lambda: T(0)),
                            8: do(lambda: V(1), lambda: T(2), lambda: S(2)),
                            9: do(lambda: V(3), lambda: T(4)), 10: do(lambda: V(5), lambda: T(6))}
                    if g:
                        mids[0] = do(lambda: V(6, before), lambda: T(7, before))
                        ends[0] = do(lambda: V(7, before), lambda: T(8, before))
                        mids[1] = do(lambda: V(8, before))
                    else:
                        mids[0] = do(lambda: stat(l, 1))
                    for i in range(GB_N):
                        n = g * GB_N + i
                        free(l, T_MIX + n)
                        products(l, B_MIX + n, n % 2, n % 2, KD, xh, xl, mid=mids.get(i),
                                 before=x_tile(l, 1) if n == 0 else None)
                        if i in ends:
                            ends[i]()

            def attn_out_start(l):
                g = GROUPS - 1
                V = lambda pos: mix_values(l, g, pos)
                T = lambda pos: turn(l, g, pos)
                for m in range(2):
                    free(l, T_ATT + m)
                    products(l, B_ATT + m, m, m, KD - 2, ah, al, last=False, done=False,
                             mid=(lambda: (V(6), T(7))) if m == 0 else (lambda: V(8)))
                    if m == 0:
                        V(7)
                        T(8)
                pe.wait_ge(o_lo, (l + 1) * GROUPS * NBAT + 1)
                for m in range(2):
                    products(l, B_ATT + m, m, m, KD, ah, al, first=False, k0=KD - 2)

            with pe.Fori(0, DEPTH) as l:
                ffn_in(l, B_IN1, T_IN1, 0)
                ffn_out(l, 0, B_OUT1, T_OUT1)
                mixer_in(l)
                attn_out_start(l)

                def ln_sum(count, done):
                    pe.wait_ge(ln_acc, l * LN_SUMS + count)
                    for h in range(2):
                        ins = mm(pstat[:, h, 0:NH], ones[:, :], acc_m[:, h * NH:(h + 1) * NH],
                                 start=True, stop=True)
                    ins.then_inc(done, 1)
                ln_sum(KD - 1, ln_mu)
                for m in range(2, KD):
                    free(l, T_ATT + m)
                    products(l, B_ATT + m, m % 2, m % 2, KD, ah, al,
                             mid=(lambda: ln_sum(LN_SUMS, ln_var)) if m == 4 else None)
                for m in range(KD):
                    free(l, T_CONV + m)
                    products(l, B_CONV + m, m % 2, m % 2, KD, xh, xl,
                             before=(lambda k: pe.wait_ge(ln_lo, l * KD + k + 1)) if m == 0 else None)
                for m in range(KD):
                    free(l, T_MO + m)
                    products(l, B_MO + m, m % 2, m % 2, KD, mh, ml,
                             before=(lambda k: pe.wait_ge(mg_lo, l * KD + k + 1)) if m == 0 else None)
                ffn_in(l, B_IN2, T_IN2, 2)
                ffn_out(l, 1, B_OUT2, T_OUT2)

            pe.wait_ge(out_taken, DEPTH * NOUT + 2)
            for i in range(4):
                s = i % 2
                if i >= 2:
                    pe.wait_ge(fin_cp, i - 1)
                for k in range(KD):
                    ins = tr(po[:, 2 * s + k // 4, (k % 4) * P:(k % 4 + 1) * P],
                             resid[:, k, META + i * P:META + (i + 1) * P], ident[:, :])
                ins.then_inc(fin_tr, 1)

        @block.vector
        def _(dve):
            tt, ts, stt = nc.vector.tensor_tensor, nc.vector.tensor_scalar, nc.vector.scalar_tensor_tensor
            flat = lambda ap: ap.rearrange("p k n -> p (k n)")

            def at(ap, m):
                return flat(ap[:, bass.ds(m, 1), :])

            for h in range(2):
                for half in range(2):
                    nc.vector.memset(halves[h * HD:(h + 1) * HD, half:half + 1], float(h == half))\
                        .then_inc(halves_done, 1)
            dve.wait_ge(pre_tr, 1)
            nc.vector.tensor_copy(prm[:, :, :].rearrange("p (a k) r -> p a k r", a=2),
                                  pstat[:, :, 0:4 * DEPTH * ROWS].rearrange("p a (k r) -> p a k r", k=4))\
                .then_inc(pre_cp, 1)
            nc.vector.tensor_copy(qk[:, :], pov[0:HD, 0:4]).then_inc(pre_cp, 1)
            dve.wait_ge(pre_cp, 2)
            tt(gkq[:, :], qk[:, 0:DEPTH], qk[:, DEPTH:], ALU.mult)
            nc.vector.memset(acc_f[:, :], 0.0).then_inc(acc_done, 2)

            def x_lo_part(l, which, m, s, gain):
                n = norm(l, which)
                sq, acc = (sq_m, acc_m) if which == 2 else (sq_f[:, :, :], acc_f[:, :])
                dve.wait_ge(x_hi, n * KD + m + 1)
                stt(at(xl, m), at(resid, m), gain, at(xh, m).bitcast(F32),
                    ALU.mult, ALU.subtract).then_inc(x_lo, 1)
                dve.wait_ge(x_sq, n * KD + m + 1)
                dve.wait_ge(acc_done, n * (KD + 2) + m + 2)
                tt(acc, acc, sq[:, s, :], ALU.add).then_inc(acc_done, 1)

            for k in range(KD + 1):
                if k < KD:
                    s = k % 2
                    dve.wait_ge(pre_tr, 2 + k)
                    nc.vector.tensor_copy(resid[:, k, META:], po[:, 2 * s, 0:512])
                    nc.vector.tensor_copy(resid[:, k, 0:META], po[:, 2 * s + 1, 0:META]).then_inc(pre_cp, 1)
                if k == KD - 1:
                    nc.vector.memset(sdif[:, :, :], 0.0).then_inc(out_taken, 2)
                if k:
                    x_lo_part(0, 0, k - 1, (k - 1) % 2, prm[:, k - 1, R_FFN1 * DEPTH:R_FFN1 * DEPTH + 1])
            nc.vector.memset(smax[:, :, :], 0.0).then_inc(o_lo, 1)

            def ready(l, n):
                dve.wait_ge(blk_used, blk(l, n) + 3)

            def rms_of(l, which):
                dve.wait_ge(std_ready, norm(l, which) + 1)
                nc.vector.reciprocal(rms[:, :], t0[:, :]).then_inc(rms_ready, 1)

            def ffn_in(l, f, n_in, t_in, which):
                rms_of(l, which)

                def step(t):
                    n = (l * 2 + f) * KF + t
                    dve.wait_ge(rms_ready, norm(l, which) + 1)
                    ready(l, n_in + 2 * t)
                    tt(two(t0[:, :]), slot(0), two(rms[:, :]), ALU.mult).then_inc(out_taken, 1)
                    dve.wait_ge(silu_done, n + 1)
                    tt(t0[:, :], t0[:, :], rms[:, :], ALU.mult).then_inc(sr_done, 1)
                    ready(l, n_in + 2 * t + 1)
                    dve.wait_ge(sr_done, n + 1)
                    tt(two(t1[:, :]), slot(1), two(t0[:, :]), ALU.mult).then_inc(out_taken, 1)
                    dve.wait_ge(h_hi, n + 1)
                    tt(at(hl, t), t1[:, :], at(hh, t).bitcast(F32), ALU.subtract).then_inc(h_lo, 1)
                with dve.Fori(0, KF) as t:
                    step(t)

            def resid_out(l, n_out, per, t_out, which, row):
                lw, ww = (l, which) if which < 3 else (l + 1, 0)
                acc = acc_m if ww == 2 else acc_f[:, :]
                nc.vector.memset(acc, 0.0).then_inc(acc_done, 2)
                with dve.Fori(0, KD // 2) as i:
                    for s in range(2):
                        m = 2 * i + s
                        ready(l, n_out + per * m + per - 1)
                        stt(two(at(resid, m)), slot(s), 0.5, two(at(resid, m)), ALU.mult, ALU.add)\
                            .then_inc(out_taken, 1)
                        gain = gnext[:, bass.ds(m, 1)] if row is None else flat(
                            lp[:, bass.ds(m, 1), row:row + 1])
                        x_lo_part(lw, ww, m, s, gain)

            def taps(l, first, last):
                for j, k in ORDER[first:last]:
                    u = ub[:, j % U_SLOTS, k:k + NT]
                    w = lp[:, j, R_CW + k:R_CW + k + 1]
                    if k == 0:
                        dve.wait_ge(u_ready, l * KD + j + 1)
                        ts(cv[:, j, :], u, w, lp[:, j, R_CB:R_CB + 1], ALU.mult, ALU.add).then_inc(conv_step, 1)
                    else:
                        dve.wait_ge(conv_step, l * KD * CONV_K + STEP_OF[j, k - 1])
                        stt(cv[:, j, :], u, w, cv[:, j, :], ALU.mult, ALU.add).then_inc(conv_step, 1)

            def take(l, g, i):
                n = g * GB_N + i
                ready(l, B_MIX + n)
                if i < 2:
                    dst = qb[:, :, i]
                elif i == 2:
                    dst = kvp[:, PAD:]
                else:
                    kind, j = FILL[g][i - 3]
                    if kind == A:
                        if j >= U_SLOTS:
                            dve.wait_ge(conv_step, l * KD * CONV_K + STEP_OF[j - U_SLOTS, CONV_K - 1])
                        stt(two(ub[:, j % U_SLOTS, CONV_K - 1:]), slot(n % 2), 0.5, two(rms[:, :]),
                            ALU.mult, ALU.mult).then_inc(out_taken, 1)
                        return
                    dst = t1[:, :] if kind == B else (ga if kind == GA else gb)[:, j, :]
                tt(two(dst), slot(n % 2), two(rms[:, :]), ALU.mult).then_inc(out_taken, 1)

            def glu(l, g, i):
                if i < 3 or FILL[g][i - 3][0] != B:
                    return 0
                j = FILL[g][i - 3][1]
                dve.wait_ge(tanh_done, l * KD + j + 1)
                u = ub[:, j % U_SLOTS, CONV_K - 1:]
                stt(u, t1[:, :], 1.0, u, ALU.add, ALU.mult).then_inc(u_ready, 1)
                return 1

            def head_rms(l, g):
                n = l * GROUPS + g
                dve.wait_ge(qstd_ready, n + 1)
                nc.vector.reciprocal(qrms[:, :, :], qstd[:, :, :]).then_inc(qrms_ready, 1)
                dve.wait_ge(kstd_ready, n + 1)
                dve.wait_ge(qrms_ready, n + 1)
                ts(nqrms[:, :, :], qrms[:, :, :], -1.0, None, ALU.mult)
                nc.vector.reciprocal(t0[0:HD, :], t0[0:HD, :]).then_inc(krms_ready, 1)
                dve.wait_ge(krms_ready, n + 1)
                stt(kn[0:HD, 0, PAD:], kvp[0:HD, PAD:], lgkq[:, :], t0[0:HD, :], ALU.mult, ALU.mult)\
                    .then_inc(kn_ready, 1)

            MAX_STEPS, DEN_STEPS = 2, 2

            def row_max(l, g, b):
                n = (l * GROUPS + g) * NBAT + b
                dve.wait_ge(s_ready, n + 1)
                if b == 0:
                    nc.vector.memset(s_win(0), NEG)
                    nc.vector.memset(s_win(1)[:, :, 0:CHUNK], NEG).then_inc(mask_done, 1)
                    dve.wait_ge(mask_done, l * GROUPS + g + 1)
                nc.vector.tensor_reduce(smax[:, :, :].rearrange("p i h -> p (i h)")
                                        .rearrange("p (b r) -> p b r", b=2), scr, AX.X,
                                        ALU.max).then_inc(max_step, 1)
                dve.wait_ge(max_step, n * MAX_STEPS + 1)
                tt(negm[:, :, :], smax[:, :, :], nqrms[:, b * SB:(b + 1) * SB, :], ALU.mult)\
                    .then_inc(max_step, 1)
                dve.wait_ge(max_step, n * MAX_STEPS + 2)
                ns = lsink[:, g:g + 1, :].to_broadcast([P, SB, 2])
                tt(negm[:, :, :], negm[:, :, :], ns, ALU.min).then_inc(neg_step, 1)
                dve.wait_ge(neg_step, n + 1)
                tt(sdif[:, :, :], negm[:, :, :], ns, ALU.subtract).then_inc(m_ready, 1)

            def norm_p(l, g, b):
                n = (l * GROUPS + g) * NBAT + b
                dve.wait_ge(exp_done, n + 1)
                tt(rden[:, :, :], psum[:, :, :], sexp[:, :, :], ALU.add).then_inc(den_step, 1)
                dve.wait_ge(den_step, DEN_STEPS * n + 1)
                nc.vector.reciprocal(rden[:, :, :], rden[:, :, :]).then_inc(den_step, 1)
                dve.wait_ge(den_step, DEN_STEPS * n + 2)
                w = pw[:, (b + 1) % 2, 0:NS].rearrange("p (t k) -> p t k", k=WK)
                rd = rden[:, :, :].rearrange("p i (h o) -> p (i h) o", o=1)
                tt(w, w, rd.to_broadcast([P, 2 * SB, WK]), ALU.mult).then_inc(p_ready, 1)

            def o_lo_part(l, g, b):
                dve.wait_ge(o_hi, (l * GROUPS + g) * NBAT + b + 1)
                a, z = tok0(b * SB), tok0(b * SB + SB - 1) + CHUNK
                src = pov[:, 0:384].rearrange("p (j n) -> p j n", j=2)[:, :, 0:z - a]
                js = slice(2 * g, 2 * g + 2)
                tt(al[:, js, a:z], src, ah[:, js, a:z].bitcast(F32), ALU.subtract).then_inc(o_lo, 1)

            with dve.Fori(0, DEPTH) as l:
                dve.wait_ge(x_sq, norm(l, 0) * KD + KD)
                dve.wait_ge(x_lo, norm(l, 0) * KD + KD)
                single = prm[:, :, 0:TB_GATE].rearrange("p k (r l) -> p k r l", l=DEPTH)
                nc.vector.tensor_copy(lp[:, :, 0:R_GA],
                                      single[:, :, :, bass.ds(l, 1)].rearrange("p k r o -> p k (r o)"))
                nc.vector.tensor_copy(lp[:, :, R_GA:R_CW], prm[:, :, bass.ds(l * 2 + TB_GATE, 2)])
                nc.vector.tensor_copy(lp[:, :, R_CW:], prm[:, :, bass.ds(l * CONV_K + TB_CONV, CONV_K)])
                nc.vector.tensor_copy(gnext[:, :], prm[:, :, bass.ds(l + R_FFN1 * DEPTH + 1, 1)].rearrange(
                    "p k o -> p (k o)"))
                nc.vector.tensor_copy(lgkq[:, :], gkq[:, bass.ds(l, 1)])
                dve.wait_ge(sink_in, PAR_SINK)
                nc.vector.tensor_copy(lsink[:, :, :], sink[:, bass.ds(l, 1), :, :].rearrange(
                    "p l g h -> p (l g) h")).then_inc(lay0, 1)
                dve.wait_ge(lay0, l + 1)
                ts(lsink[:, :, :], lsink[:, :, :], -1.0, None, ALU.mult)
                ts(lp[:, :, R_GA:R_GB + 1], lp[:, :, R_GA:R_GB + 1], 0.5, None, ALU.mult).then_inc(lay, 1)
                dve.wait_ge(lay, l + 1)

                ffn_in(l, 0, B_IN1, T_IN1, 0)
                resid_out(l, B_OUT1, 2, T_OUT1, 1, R_MIX)

                nc.vector.memset(ub[:, :, 0:CONV_K - 1], 0.0)
                nc.vector.memset(kvp[:, 0:PAD], 0.0)
                nc.vector.memset(kn[:, :, 0:PAD], 0.0)
                nc.vector.memset(kn[HD:P, 0, PAD:], 0.0)
                nc.vector.memset(kn[0:HD, 1, PAD:], 0.0)
                nc.vector.memset(vm[:, :], 0.0)
                rms_of(l, 1)
                dve.wait_ge(rms_ready, norm(l, 1) + 1)
                tap, inputs = 0, 0
                for g in range(GROUPS):
                    for i in range(GB_N):
                        if i == 9:
                            o_lo_part(l, g, 0)
                        take(l, g, i)
                        if i == 1 and g:
                            o_lo_part(l, g - 1, 2)
                        if i == 3:
                            head_rms(l, g)
                        if i == 5:
                            row_max(l, g, 0)
                        if i == 6:
                            norm_p(l, g, 0)
                        if i == 8:
                            norm_p(l, g, 1)
                            row_max(l, g, 2)
                        if i == 10:
                            o_lo_part(l, g, 1)
                        n = tap
                        while n < min(tap + TAPS[i], len(ORDER)) and ORDER[n][0] < inputs:
                            n += 1
                        taps(l, tap, n)
                        tap = n
                        inputs += glu(l, g, i)
                        if i == 6:
                            row_max(l, g, 1)
                        if i == 9:
                            norm_p(l, g, 2)

                def take_att(m):
                    ready(l, B_ATT + m)
                    stt(two(gb[:, m, :]), two(gb[:, m, :]), 1.0, slot(m % 2), ALU.add, ALU.mult)\
                        .then_inc(out_taken, 1)
                late = len(ORDER) - tap
                taps(l, tap, tap + min(late, LATE))
                if late > LATE:
                    o_lo_part(l, GROUPS - 1, 2)
                    taps(l, tap + LATE, len(ORDER))
                dve.wait_ge(conv_step, (l + 1) * KD * CONV_K)
                n = l * LN_SUMS
                for k in range(1, KD):
                    if k > 1:
                        dve.wait_ge(ln_acc, n + k - 1)
                    tt(acc_m, cv[:, 0, :] if k == 1 else acc_m, cv[:, k, :], ALU.add).then_inc(ln_acc, 1)
                    if k == max(1, min(LATE - late, KD - 1)) and late <= LATE:
                        o_lo_part(l, GROUPS - 1, 2)
                take_att(0)
                take_att(1)
                dve.wait_ge(ln_mu, l + 1)
                for k in range(KD + 1):
                    if k < KD:
                        stt(two(cv[:, k, :]), pstat[:, :, 0:NH], -1.0 / D, two(cv[:, k, :]), ALU.mult,
                            ALU.add).then_inc(ln_d, 1)
                    if k:
                        dve.wait_ge(ln_sq, l * KD + k)
                        if k == 1:
                            nc.vector.tensor_copy(acc_m, sq_m[:, 0, :]).then_inc(ln_acc, 1)
                        else:
                            dve.wait_ge(ln_acc, n + KD - 1 + k - 1)
                            tt(acc_m, acc_m, sq_m[:, (k - 1) % 2, :], ALU.add).then_inc(ln_acc, 1)
                    if k == 4:
                        take_att(2)
                take_att(3)
                dve.wait_ge(ln_std, l + 1)
                nc.vector.reciprocal(rms[:, :], t0[:, :]).then_inc(ln_r, 1)
                dve.wait_ge(ln_r, l + 1)
                take_att(4)
                for k in range(KD + 1):
                    if k < KD:
                        tt(cv[:, k, :], cv[:, k, :], rms[:, :], ALU.mult).then_inc(ln_y, 1)
                    if k:
                        dve.wait_ge(ln_hi, l * KD + k)
                        tt(xl[:, k - 1, :], cv[:, k - 1, :], xh[:, k - 1, :].bitcast(F32), ALU.subtract)\
                            .then_inc(ln_lo, 1)
                    if k == 3:
                        take_att(5)
                take_att(6)
                take_att(7)
                for m in range(KD):
                    ready(l, B_CONV + m)
                    if m:
                        dve.wait_ge(mg_lo, l * KD + m)
                    stt(two(t1[:, :]), two(ga[:, m, :]), 1.0, slot(m % 2), ALU.add, ALU.mult)\
                        .then_inc(out_taken, 1)
                    dve.wait_ge(out_taken, tile(l, T_CONV) + m + 3)
                    tt(t1[:, :], t1[:, :], gb[:, m, :], ALU.add).then_inc(mg_sum, 1)
                    dve.wait_ge(mg_hi, l * KD + m + 1)
                    tt(ml[:, m, :], t1[:, :], mh[:, m, :].bitcast(F32), ALU.subtract).then_inc(mg_lo, 1)
                resid_out(l, B_MO, 1, T_MO, 2, R_FFN2)
                ffn_in(l, 1, B_IN2, T_IN2, 2)
                resid_out(l, B_OUT2, 2, T_OUT2, 3, None)

            for i in range(4):
                dve.wait_ge(fin_tr, i + 1)
                nc.vector.tensor_copy(yout[:, i, :].rearrange("p (a n) -> p a n", a=2),
                                      po[:, 2 * (i % 2):2 * (i % 2) + 2, :]).then_inc(fin_cp, 1)


_INS = ["x", "meta_tokens", "ffn1_norm", "ffn1_w_in", "ffn1_w_out", "mix_norm", "w_in", "gate_bias",
        "conv_w", "conv_b", "conv_ln_g", "conv_ln_b", "conv_w_out", "q_norm", "k_norm", "attn_sinks",
        "attn_w_out", "w_out", "ffn2_norm", "ffn2_w_in", "ffn2_w_out"]


def kernel(**inputs):
    import numpy as np
    import concourse.bacc as bacc
    from concourse.bass_utils import run_bass_kernel_spmd

    nc = bacc.Bacc("TRN2", target_bir_lowering=False, num_devices=1)
    arrays, args = {}, []
    for name in _INS:
        a = np.ascontiguousarray(inputs[name])
        arrays[f"in_{name}"] = a
        args.append(nc.dram_tensor(f"in_{name}", a.shape, mybir.dt.from_np(a.dtype), kind="ExternalInput").ap())
    out = nc.dram_tensor("out_0", (1, SEQ, D), F32, kind="ExternalOutput").ap()
    build(nc, *args, out)
    r = run_bass_kernel_spmd(nc, [arrays], core_ids=[0])
    return r.results[0]["out_0"]
```
